# Optimizing a Trainium2 kernel written in Bass

```python
import math
import jax
import jax.numpy as jnp
from jax import lax
import numpy as np

D_MODEL = 1024
BATCH = 1
SEQ = 256
DEPTH = 2

A_HEADS = 8
A_KV_HEADS = 2
A_HEAD_DIM = 64
A_WIDTH = A_HEADS * A_HEAD_DIM
IDX_HEADS = 8
IDX_DIM = 32
TOPK_MAX = 256
Q_BLOCK = 128
ROPE_THETA = 500000.0
ROPE_FRACTION = 4
SC_WIDTH = 512
SC_CONV = 3
RW_HEADS = 8
RW_HEAD_DIM = 64
RW_WIDTH = RW_HEADS * RW_HEAD_DIM
RW_W_LORA = 64
RW_A_LORA = 64
RW_G_LORA = 128
RW_IN = 3 * RW_WIDTH + RW_W_LORA + RW_A_LORA + RW_G_LORA
RW_GN_EPS = 64e-5
N_BRANCH = 3
BRANCH_WIDTH = 512
D_FF = 2816
FFN_CONV = 3
RMS_EPS = 1e-6
POS_OFFSET_MAX = 4096

IN_SIZES = (A_WIDTH, A_KV_HEADS * A_HEAD_DIM, A_KV_HEADS * A_HEAD_DIM,
            IDX_HEADS * IDX_DIM, IDX_DIM, IDX_HEADS,
            SC_WIDTH, SC_WIDTH, SC_WIDTH,
            RW_IN,
            N_BRANCH * D_MODEL)
N_IN = sum(IN_SIZES)


def rms_norm(x, g):
    xf = x.astype(jnp.float32)
    y = xf * lax.rsqrt(jnp.mean(xf * xf, axis=-1, keepdims=True) + RMS_EPS)
    return (y * g.astype(jnp.float32)).astype(x.dtype)

def partial_rope(x, pos):
    dh = x.shape[-1]
    rot = dh // ROPE_FRACTION
    half = rot // 2
    inv = ROPE_THETA ** (-jnp.arange(half, dtype=jnp.float32) * 2.0 / rot)
    ang = pos.astype(jnp.float32)[:, :, None] * inv
    cos = jnp.cos(ang)[:, :, None, :]
    sin = jnp.sin(ang)[:, :, None, :]
    xf = x.astype(jnp.float32)
    x1 = xf[..., :half]
    x2 = xf[..., half:rot]
    out = jnp.concatenate([x1 * cos - x2 * sin, x2 * cos + x1 * sin, xf[..., rot:]], axis=-1)
    return out.astype(x.dtype)

def causal_dwconv(u, w):
    width = w.shape[0]
    seq = u.shape[1]
    up = jnp.pad(u, ((0, 0), (width - 1, 0), (0, 0)))
    out = up[:, 0:seq] * w[0]
    for j in range(1, width):
        out = out + up[:, j:j + seq] * w[j]
    return out

def dsa_attention(q, k, v, qi, ki, wi):
    bsz, seq = q.shape[0], q.shape[1]
    k_sel = min(TOPK_MAX, seq // 4)
    n_blk = seq // Q_BLOCK
    group = A_HEADS // A_KV_HEADS
    scale = A_HEAD_DIM ** -0.5
    idx_scale = (IDX_HEADS ** -0.5) * (IDX_DIM ** -0.5)
    b_idx = jnp.arange(bsz)[:, None, None]
    key_pos = jnp.arange(seq)

    def block(i):
        t0 = i * Q_BLOCK
        q_b = lax.dynamic_slice_in_dim(q, t0, Q_BLOCK, axis=1)
        qi_b = lax.dynamic_slice_in_dim(qi, t0, Q_BLOCK, axis=1)
        wi_b = lax.dynamic_slice_in_dim(wi, t0, Q_BLOCK, axis=1)
        t_pos = t0 + jnp.arange(Q_BLOCK)
        causal = key_pos[None, :] <= t_pos[:, None]
        rel = jax.nn.relu(jnp.einsum('bthd,bsd->bths', qi_b, ki).astype(jnp.float32))
        isc = jnp.einsum('bths,bth->bts', rel, wi_b.astype(jnp.float32) * idx_scale)
        isc = jnp.where(causal[None], isc, -jnp.inf)
        _, sel = lax.top_k(isc, k_sel)
        valid = sel <= t_pos[None, :, None]
        k_g = k[b_idx, sel]
        v_g = v[b_idx, sel]
        q_g = q_b.reshape(bsz, Q_BLOCK, A_KV_HEADS, group, A_HEAD_DIM)
        s = jnp.einsum('btngd,btknd->btngk', q_g, k_g).astype(jnp.float32) * scale
        s = jnp.where(valid[:, :, None, None, :], s, -jnp.inf)
        p = jax.nn.softmax(s, axis=-1).astype(v.dtype)
        o = jnp.einsum('btngk,btknd->btngd', p, v_g)
        return o.reshape(bsz, Q_BLOCK, A_WIDTH)

    out = lax.map(block, jnp.arange(n_blk))
    return out.transpose(1, 0, 2, 3).reshape(bsz, seq, A_WIDTH)

def short_conv_mixer(u, sc_b, sc_c, w_conv):
    return sc_b * causal_dwconv(sc_c * u, w_conv)

def rwkv7_time_mix(z, mu, w0, w_up, a0, a_up, g_up, k_k, k_a, r_k, ln_w, ln_b):
    bsz, seq = z.shape[0], z.shape[1]
    f32 = jnp.float32
    z_prev = jnp.pad(z, ((0, 0), (1, 0), (0, 0)))[:, :seq]
    z = z + (z_prev - z) * mu
    r, k, v, lw, la, lg = jnp.split(
        z, [RW_WIDTH, 2 * RW_WIDTH, 3 * RW_WIDTH, 3 * RW_WIDTH + RW_W_LORA,
            3 * RW_WIDTH + RW_W_LORA + RW_A_LORA], axis=-1)
    zw = (w0 + jnp.tanh(lw) @ w_up).astype(f32)
    decay = jnp.exp(-math.exp(-0.5) * jax.nn.sigmoid(zw))
    a = jax.nn.sigmoid((a0 + la @ a_up).astype(f32))
    g = (jax.nn.sigmoid(lg) @ g_up).astype(f32)
    hs = (bsz, seq, RW_HEADS, RW_HEAD_DIM)
    r = r.astype(f32).reshape(hs)
    v = v.astype(f32).reshape(hs)
    kf = k.astype(f32)
    decay = decay.reshape(hs)
    a = a.reshape(hs)
    kk = (kf * k_k.astype(f32)).reshape(hs)
    kk = kk * lax.rsqrt(jnp.maximum(jnp.sum(kk * kk, axis=-1, keepdims=True), 1e-24))
    kf = (kf * (1.0 + (a.reshape(bsz, seq, RW_WIDTH) - 1.0) * k_a.astype(f32))).reshape(hs)

    def step(state, inp):
        r_t, w_t, k_t, v_t, ka_t, kb_t = inp
        sa = jnp.einsum('bhvk,bhk->bhv', state, ka_t)
        state = (state * w_t[:, :, None, :] + sa[..., None] * kb_t[:, :, None, :]
                 + v_t[..., None] * k_t[:, :, None, :])
        y_t = jnp.einsum('bhvk,bhk->bhv', state, r_t)
        return state, y_t

    tm = lambda t: jnp.swapaxes(t, 0, 1)
    xs = (tm(r), tm(decay), tm(kf), tm(v), tm(-kk), tm(kk * a))
    s0 = jnp.zeros((bsz, RW_HEADS, RW_HEAD_DIM, RW_HEAD_DIM), f32)
    _, y = lax.scan(step, s0, xs)
    y = jnp.swapaxes(y, 0, 1)
    mean = jnp.mean(y, axis=-1, keepdims=True)
    var = jnp.mean(jnp.square(y - mean), axis=-1, keepdims=True)
    yn = ((y - mean) * lax.rsqrt(var + RW_GN_EPS) * ln_w.astype(f32).reshape(RW_HEADS, RW_HEAD_DIM)
          + ln_b.astype(f32).reshape(RW_HEADS, RW_HEAD_DIM))
    bonus = jnp.sum(r * kf * r_k.astype(f32), axis=-1, keepdims=True) * v
    out = (yn + bonus) * g.reshape(hs)
    return out.reshape(bsz, seq, RW_WIDTH).astype(z.dtype)

def conv_glu_ffn(x, w_up, w_conv, w_down):
    u = causal_dwconv(x @ w_up, w_conv)
    gate, up = jnp.split(u, 2, axis=-1)
    return (jax.nn.silu(gate) * up) @ w_down

def first_inputs(seed: int = 0) -> dict:
    key = jax.random.key(seed)
    ks = jax.random.split(key, 26)
    f32 = jnp.float32

    def nrm(k, shape, scale):
        return jax.random.normal(k, shape, f32) * scale

    L = DEPTH
    x = nrm(ks[0], (BATCH, SEQ, D_MODEL), 1.0)
    positions = (jax.random.randint(ks[1], (BATCH, 1), 0, POS_OFFSET_MAX, dtype=jnp.int32)
                 + jnp.arange(SEQ, dtype=jnp.int32)[None, :])
    return {
        'x': x,
        'positions': positions,
        'norm_mix': 1.0 + nrm(ks[2], (L, D_MODEL), 0.02),
        'w_in': nrm(ks[3], (L, D_MODEL, N_IN), D_MODEL ** -0.5),
        'b_gate': nrm(ks[4], (L, N_BRANCH * D_MODEL), 0.02),
        'sc_conv': nrm(ks[5], (L, SC_CONV, SC_WIDTH), SC_CONV ** -0.5),
        'rw_mu': jax.random.uniform(ks[6], (L, RW_IN), f32),
        'rw_w0': -1.0 + nrm(ks[7], (L, RW_WIDTH), 0.5),
        'rw_w_up': nrm(ks[8], (L, RW_W_LORA, RW_WIDTH), 0.5 * RW_W_LORA ** -0.5),
        'rw_a0': nrm(ks[9], (L, RW_WIDTH), 0.1),
        'rw_a_up': nrm(ks[10], (L, RW_A_LORA, RW_WIDTH), 0.5 * RW_A_LORA ** -0.5),
        'rw_g_up': nrm(ks[11], (L, RW_G_LORA, RW_WIDTH), RW_G_LORA ** -0.5),
        'rw_k_k': 0.85 + nrm(ks[12], (L, RW_WIDTH), 0.05),
        'rw_k_a': 1.0 + nrm(ks[13], (L, RW_WIDTH), 0.05),
        'rw_r_k': nrm(ks[14], (L, RW_HEADS, RW_HEAD_DIM), 0.1),
        'rw_ln_w': 1.0 + nrm(ks[15], (L, RW_WIDTH), 0.02),
        'rw_ln_b': nrm(ks[16], (L, RW_WIDTH), 0.02),
        'w_branch': nrm(ks[17], (L, N_BRANCH, BRANCH_WIDTH, D_MODEL), BRANCH_WIDTH ** -0.5),
        'w_out': nrm(ks[18], (L, D_MODEL, D_MODEL), D_MODEL ** -0.5),
        'norm_ffn': 1.0 + nrm(ks[19], (L, D_MODEL), 0.02),
        'ffn_up': nrm(ks[20], (L, D_MODEL, 2 * D_FF), D_MODEL ** -0.5),
        'ffn_conv': nrm(ks[21], (L, FFN_CONV, 2 * D_FF), FFN_CONV ** -0.5),
        'ffn_down': nrm(ks[22], (L, D_FF, D_MODEL), D_FF ** -0.5),
        'norm_final': 1.0 + nrm(ks[23], (D_MODEL,), 0.02),
    }

def first_block(x, positions, norm_mix, w_in, b_gate, sc_conv, rw_mu, rw_w0, rw_w_up, rw_a0,
              rw_a_up, rw_g_up, rw_k_k, rw_k_a, rw_r_k, rw_ln_w, rw_ln_b, w_branch, w_out,
              norm_ffn, ffn_up, ffn_conv, ffn_down, norm_final):
    bsz, seq = x.shape[0], x.shape[1]
    split_points = [int(p) for p in np.cumsum(IN_SIZES)[:-1]]
    h = x
    for l in range(DEPTH):
        xn = rms_norm(h, norm_mix[l])
        proj = xn @ w_in[l]
        (q, k, v, qi, ki, wi, sc_u, sc_b, sc_c, rw_z, gate_pre) = jnp.split(proj, split_points, axis=-1)
        q = partial_rope(q.reshape(bsz, seq, A_HEADS, A_HEAD_DIM), positions)
        k = partial_rope(k.reshape(bsz, seq, A_KV_HEADS, A_HEAD_DIM), positions)
        v = v.reshape(bsz, seq, A_KV_HEADS, A_HEAD_DIM)
        qi = partial_rope(qi.reshape(bsz, seq, IDX_HEADS, IDX_DIM), positions)
        ki = partial_rope(ki.reshape(bsz, seq, 1, IDX_DIM), positions)[:, :, 0]
        y_a = dsa_attention(q, k, v, qi, ki, wi)
        y_b = short_conv_mixer(sc_u, sc_b, sc_c, sc_conv[l])
        y_c = rwkv7_time_mix(rw_z, rw_mu[l], rw_w0[l], rw_w_up[l], rw_a0[l], rw_a_up[l],
                             rw_g_up[l], rw_k_k[l], rw_k_a[l], rw_r_k[l], rw_ln_w[l], rw_ln_b[l])
        branches = jnp.stack([y_a, y_b, y_c], axis=2)
        up = jnp.einsum('bsgc,gcd->bsgd', branches, w_branch[l])
        gates = jax.nn.sigmoid(gate_pre + b_gate[l]).reshape(bsz, seq, N_BRANCH, D_MODEL)
        mixed = jnp.sum(gates * up, axis=2)
        h = h + mixed @ w_out[l]
        h = h + conv_glu_ffn(rms_norm(h, norm_ffn[l]), ffn_up[l], ffn_conv[l], ffn_down[l])
    return rms_norm(h, norm_final)


HEAD_DIM = 64
A_HEADS_2 = 16
A_WIDTH_2 = A_HEADS_2 * HEAD_DIM
DILATED_PAIRS = ((128, 1), (512, 4), (2048, 16))
B_HEADS = D_MODEL // (2 * HEAD_DIM)
B_QK_WIDTH = 2 * B_HEADS * HEAD_DIM
B_V_DIM = 2 * HEAD_DIM
B_WIDTH = B_HEADS * B_V_DIM
IN_WIDTHS = (A_WIDTH_2, A_WIDTH_2, A_WIDTH_2, A_WIDTH_2,
             B_QK_WIDTH, B_QK_WIDTH, B_WIDTH, B_WIDTH,
             D_MODEL, D_MODEL)
IN_TOTAL = sum(IN_WIDTHS)
ROPE_DIM = HEAD_DIM // 4
SUBLN_EPS = 1e-5
NEG = -1e30


def rms_norm_2(x, w, eps):
    xf = x.astype(jnp.float32)
    return xf * lax.rsqrt(jnp.mean(xf * xf, axis=-1, keepdims=True) + eps) * w.astype(jnp.float32)

def rope_tables(seq):
    inv = 1.0 / (ROPE_THETA ** (jnp.arange(0, ROPE_DIM, 2, dtype=jnp.float32) / ROPE_DIM))
    ang = jnp.arange(seq, dtype=jnp.float32)[:, None] * inv[None, :]
    return jnp.cos(ang), jnp.sin(ang)

def partial_rope_2(t, cos, sin):
    half = ROPE_DIM // 2
    tr = t[..., :ROPE_DIM].astype(jnp.float32)
    t1, t2 = tr[..., :half], tr[..., half:]
    c = cos[None, :, None, :]
    s = sin[None, :, None, :]
    rot = jnp.concatenate([t1 * c - t2 * s, t1 * s + t2 * c], axis=-1).astype(t.dtype)
    return jnp.concatenate([rot, t[..., ROPE_DIM:]], axis=-1)

def split_cols(u):
    outs = []
    start = 0
    for w in IN_WIDTHS:
        outs.append(u[..., start:start + w])
        start += w
    return outs

def dilated_pattern(q, k, v, window, dilation):
    b, s, h, dh = q.shape
    n = window // dilation
    chunk = dilation * n
    sp = -(-s // chunk) * chunk
    length = sp // dilation
    nb = length // n

    def to_blocks(t):
        t = jnp.pad(t, ((0, 0), (0, sp - s), (0, 0), (0, 0)))
        t = t.reshape(b, length, dilation, h, dh).transpose(0, 2, 1, 3, 4)
        return t.reshape(b, dilation, nb, n, h, dh)

    def with_prev(t):
        prev = jnp.pad(t, ((0, 0), (0, 0), (1, 0), (0, 0), (0, 0), (0, 0)))[:, :, :-1]
        return jnp.concatenate([prev, t], axis=3)

    qb = to_blocks(q)
    kb = with_prev(to_blocks(k))
    vb = with_prev(to_blocks(v))
    scores = jnp.einsum('brnqhd,brnkhd->brnqhk', qb, kb,
                        preferred_element_type=jnp.float32) * (HEAD_DIM ** -0.5)
    qi = jnp.arange(n)[:, None]
    kc = jnp.arange(2 * n)[None, :]
    dist = qi + n - kc
    blk = jnp.arange(nb)[:, None, None]
    valid = (dist >= 0) & (dist <= n) & (blk * n + kc - n >= 0)
    scores = jnp.where(valid[None, None, :, :, None, :], scores, NEG)
    m = jnp.max(scores, axis=-1)
    p = jnp.exp(scores - m[..., None])
    den = jnp.sum(p, axis=-1)
    o = jnp.einsum('brnqhk,brnkhd->brnqhd', p, vb.astype(jnp.float32)) / den[..., None]

    def from_blocks(t):
        t = t.reshape((b, dilation, length) + t.shape[4:])
        t = jnp.swapaxes(t, 1, 2)
        return t.reshape((b, sp) + t.shape[3:])[:, :s]

    return from_blocks(o), from_blocks(m), from_blocks(den)

def dilated_mixture(q, k, v):
    outs = [dilated_pattern(q, k, v, w, d) for (w, d) in DILATED_PAIRS]
    m_all = jnp.stack([r[1] for r in outs])
    d_all = jnp.stack([r[2] for r in outs])
    o_all = jnp.stack([r[0] for r in outs])
    wts = d_all * jnp.exp(m_all - jnp.max(m_all, axis=0))
    return jnp.sum(wts[..., None] * o_all, axis=0) / jnp.sum(wts, axis=0)[..., None]

def diff_attention(q1, q2, k1, k2, v, lam):
    b, s, h, dh = q1.shape
    nq = s // Q_BLOCK
    qs = jnp.stack([q1, q2], 0).reshape(2, b, nq, Q_BLOCK, h, dh).transpose(2, 0, 1, 3, 4, 5)
    ks = jnp.stack([k1, k2], 0)
    vf = v.astype(jnp.float32)
    kpos = jnp.arange(s)

    def one_block(args):
        qblk, bi = args
        sc = jnp.einsum('mbqhd,mbkhd->mbhqk', qblk, ks,
                        preferred_element_type=jnp.float32) * (dh ** -0.5)
        qpos = bi * Q_BLOCK + jnp.arange(Q_BLOCK)
        sc = jnp.where(kpos[None, :] <= qpos[:, None], sc, NEG)
        p = jax.nn.softmax(sc, axis=-1)
        a = p[0] - lam * p[1]
        return jnp.einsum('bhqk,bkhe->bqhe', a, vf)

    out = lax.map(one_block, (qs, jnp.arange(nq)))
    return out.transpose(1, 0, 2, 3, 4).reshape(b, s, h, 2 * dh)

def lambda_init_value(layer):
    return 0.8 - 0.6 * math.exp(-0.3 * layer)

def hybrid_layer(x, layer, norm_w, w_in, lq1, lk1, lq2, lk2, subln_w,
                 w_proj_a, w_proj_b, w_out, cos, sin):
    b, s, _ = x.shape
    hdn = rms_norm_2(x, norm_w, RMS_EPS).astype(x.dtype)
    u = hdn @ w_in
    qa, ka, va, za, qb, kb, vb, zb, ga, gb = split_cols(u)

    qa = partial_rope_2(qa.reshape(b, s, A_HEADS_2, HEAD_DIM), cos, sin)
    ka = partial_rope_2(ka.reshape(b, s, A_HEADS_2, HEAD_DIM), cos, sin)
    va = va.reshape(b, s, A_HEADS_2, HEAD_DIM)
    ya = dilated_mixture(qa, ka, va).reshape(b, s, A_WIDTH_2)
    ya = ya * jax.nn.silu(za.astype(jnp.float32))

    qb = partial_rope_2(qb.reshape(b, s, 2 * B_HEADS, HEAD_DIM), cos, sin)
    kb = partial_rope_2(kb.reshape(b, s, 2 * B_HEADS, HEAD_DIM), cos, sin)
    vb = vb.reshape(b, s, B_HEADS, B_V_DIM)
    lam_init = lambda_init_value(layer)
    lam = (jnp.exp(jnp.sum(lq1.astype(jnp.float32) * lk1.astype(jnp.float32)))
           - jnp.exp(jnp.sum(lq2.astype(jnp.float32) * lk2.astype(jnp.float32))) + lam_init)
    ob = diff_attention(qb[:, :, 0::2], qb[:, :, 1::2], kb[:, :, 0::2], kb[:, :, 1::2], vb, lam)
    ob = rms_norm_2(ob, subln_w, SUBLN_EPS) * (1.0 - lam_init)
    yb = ob.reshape(b, s, B_WIDTH) * jax.nn.silu(zb.astype(jnp.float32))

    pa = ya.astype(x.dtype) @ w_proj_a
    pb = yb.astype(x.dtype) @ w_proj_b
    merged = (jax.nn.sigmoid(ga.astype(jnp.float32)) * pa.astype(jnp.float32)
              + jax.nn.sigmoid(gb.astype(jnp.float32)) * pb.astype(jnp.float32))
    return x + (merged.astype(x.dtype) @ w_out).astype(x.dtype)

def second_inputs(seed: int = 0) -> dict:
    key = jax.random.key(seed)
    ks = jax.random.split(key, 16)
    f32 = jnp.float32
    x = jax.random.normal(ks[0], (BATCH, SEQ, D_MODEL), f32)
    norm_w = 1.0 + 0.02 * jax.random.normal(ks[1], (DEPTH, D_MODEL), f32)
    w_in = jax.random.normal(ks[2], (DEPTH, D_MODEL, IN_TOTAL), f32) * D_MODEL ** -0.5
    lambda_q1 = 0.1 * jax.random.normal(ks[3], (DEPTH, HEAD_DIM), f32)
    lambda_k1 = 0.1 * jax.random.normal(ks[4], (DEPTH, HEAD_DIM), f32)
    lambda_q2 = 0.1 * jax.random.normal(ks[5], (DEPTH, HEAD_DIM), f32)
    lambda_k2 = 0.1 * jax.random.normal(ks[6], (DEPTH, HEAD_DIM), f32)
    subln_w = 1.0 + 0.02 * jax.random.normal(ks[7], (DEPTH, B_V_DIM), f32)
    w_proj_a = jax.random.normal(ks[8], (DEPTH, A_WIDTH_2, D_MODEL), f32) * A_WIDTH_2 ** -0.5
    w_proj_b = jax.random.normal(ks[9], (DEPTH, B_WIDTH, D_MODEL), f32) * B_WIDTH ** -0.5
    w_out = jax.random.normal(ks[10], (DEPTH, D_MODEL, D_MODEL), f32) * D_MODEL ** -0.5
    final_norm_w = 1.0 + 0.02 * jax.random.normal(ks[11], (D_MODEL,), f32)
    return {'x': x, 'norm_w': norm_w, 'w_in': w_in,
            'lambda_q1': lambda_q1, 'lambda_k1': lambda_k1,
            'lambda_q2': lambda_q2, 'lambda_k2': lambda_k2,
            'subln_w': subln_w, 'w_proj_a': w_proj_a, 'w_proj_b': w_proj_b,
            'w_out': w_out, 'final_norm_w': final_norm_w}

def second_block(x, norm_w, w_in, lambda_q1, lambda_k1, lambda_q2, lambda_k2,
              subln_w, w_proj_a, w_proj_b, w_out, final_norm_w):
    cos, sin = rope_tables(x.shape[1])
    h = x
    for layer in range(DEPTH):
        h = hybrid_layer(h, layer, norm_w[layer], w_in[layer],
                         lambda_q1[layer], lambda_k1[layer], lambda_q2[layer], lambda_k2[layer],
                         subln_w[layer], w_proj_a[layer], w_proj_b[layer], w_out[layer],
                         cos, sin)
    return rms_norm_2(h, final_norm_w, RMS_EPS).astype(x.dtype)


def setup_inputs(seed=0):
    out = dict(first_inputs(seed))
    for name, value in second_inputs(seed + 1).items():
        if name != "x":
            out[name + "_2"] = value
    return out


def reference(
    x, positions, norm_mix, w_in, b_gate, sc_conv, rw_mu, rw_w0, rw_w_up, rw_a0, rw_a_up,
    rw_g_up, rw_k_k, rw_k_a, rw_r_k, rw_ln_w, rw_ln_b, w_branch, w_out, norm_ffn, ffn_up,
    ffn_conv, ffn_down, norm_final, norm_w_2, w_in_2, lambda_q1_2, lambda_k1_2, lambda_q2_2,
    lambda_k2_2, subln_w_2, w_proj_a_2, w_proj_b_2, w_out_2, final_norm_w_2,
):
    x = first_block(
        x, positions, norm_mix, w_in, b_gate, sc_conv, rw_mu, rw_w0, rw_w_up, rw_a0, rw_a_up,
        rw_g_up, rw_k_k, rw_k_a, rw_r_k, rw_ln_w, rw_ln_b, w_branch, w_out, norm_ffn, ffn_up,
        ffn_conv, ffn_down, norm_final,
    )
    return second_block(
        x, norm_w_2, w_in_2, lambda_q1_2, lambda_k1_2, lambda_q2_2, lambda_k2_2, subln_w_2,
        w_proj_a_2, w_proj_b_2, w_out_2, final_norm_w_2,
    )


_drawn_inputs = setup_inputs


def setup_inputs(seed=0):
    import zlib

    import numpy as np

    out = dict(_drawn_inputs(seed))
    spreads = {}
    factors = {'b_gate': 5.366,
     'rw_k_k': 6.414,
     'rw_ln_w': 4.995,
     'rw_ln_b': 3.936,
     'norm_w_2': 4.013,
     'lambda_k1_2': 3.194,
     'subln_w_2': 8.0}
    for name, (base, spread) in spreads.items():
        noise = np.random.default_rng([zlib.crc32(name.encode()), seed]).standard_normal(out[name].shape)
        drawn = base * np.exp(spread * noise) if base else spread * noise
        out[name] = jnp.asarray(drawn.astype(out[name].dtype))
    for name, factor in factors.items():
        out[name] = (out[name] * factor).astype(out[name].dtype)
    return out
```

```python
import math
from contextlib import ExitStack

import numpy as np

import concourse.bass as bass
from concourse import mybir

F32 = mybir.dt.float32
F32R = mybir.dt.float32r
I32 = mybir.dt.int32
ALU = mybir.AluOpType
ACT = mybir.ActivationFunctionType
AX_X = mybir.AxisListType.X

P = 128
T = 256
D = 1024
KD = D // P
LAYERS = 2
D_FF = 2816
FT = D_FF // P
HD = 64
IDX_HEADS, IDX_DIM = 8, 32
TOPK = T // 4
RMS_EPS = 1e-6
SUBLN_EPS = 1e-5
GN_EPS = 64e-5
DECAY = math.exp(-0.5)
NEG = -1e30
TAKEN = -3e38
CH = 64
NCH = T // CH
SUB = 16
TWO_PI = 2.0 * math.pi

Q0, K0, V0, QI0, KI0, U0, B0, C0, RW0, GATE0, N_IN = 0, 512, 640, 768, 1024, 1064, 1576, 2088, 2600, 4392, 7464

UNITS_A = ([("q", 0), ("q", 1), ("kv", 0), ("qi", 0), ("ki", 0)] + [("rz", i) for i in range(7)]
           + [("uc", i) for i in range(4)] + [("cb", i) for i in range(2)]
           + [("ga", i) for i in range(4)] + [("gb", i) for i in range(4)]
           + [("br0", i) for i in range(2)] + [("br1", i) for i in range(2)]
           + [("gc", i) for i in range(4)] + [("br2", i) for i in range(2)]
           + [("out", i) for i in range(4)])
LAG_DOWN = 2


def ffn_units():
    units = []
    for pair in range(FT // 2 + LAG_DOWN):
        if pair < FT // 2:
            units += [("up", 2 * pair), ("up", 2 * pair + 1)]
        if pair >= LAG_DOWN:
            units.append(("down", pair - LAG_DOWN))
    return units


UNITS_A += ffn_units()
UNITS_B = ([("v", i) for i in range(4)] + [("qk", i) for i in range(8)] + [("z", i) for i in range(4)]
           + [("V", i) for i in range(4)] + [("QK", i) for i in range(8)] + [("Z", i) for i in range(4)]
           + [("g", i) for i in range(4)] + [("G", i) for i in range(4)]
           + [("pa", i) for i in range(4)] + [("pb", i) for i in range(4)] + [("out", i) for i in range(4)])

def offsets(sizes):
    table, at = {}, 0
    for name, n in sizes:
        table[name] = at
        at += n
    return table, at


VA, NVA = offsets([("norm", KD), ("ffn_norm", KD), ("b_gate", 24), ("sc", 12), ("mu", 14), ("w0", 4), ("a0", 4),
                   ("k_k", 4), ("k_a", 4), ("r_k", 4), ("ln_w", 4), ("ln_b", 4), ("conv", 6 * FT)])
VB, NVB = offsets([("norm", KD), ("subln", 1), ("lam", 4), ("lam_init", 2)])
CC, NCC = offsets([("ident", P), ("ones", P), ("blk", P), ("rot64", P), ("causal", T), ("final", 2 * KD)])
CA, NCA = offsets([("rot32", P), ("rep", 224), ("dup", 512), ("inv64", 1), ("inv32", 1), ("gmask", 2 * CH),
                   ("off", CH), ("sel", 32), ("spread", 512)])
CB, NCB = offsets([("dilated", 384), ("cos", T), ("sin", T)])


class Tally:

    def __init__(self, sem):
        self.sem, self.n, self.seen = sem, 0, {}

    def take(self, eng, k=1):
        self.seen[id(eng)] = self.seen.get(id(eng), 0) + k
        eng.wait_ge(self.sem, self.seen[id(eng)])

    def at_least(self, eng, n):
        if n > 0:
            eng.wait_ge(self.sem, n)

    def restart(self):
        self.n, self.seen = 0, {}


class Line:

    def __init__(self, eng, steps):
        self.eng, self.steps, self.last = eng, steps, None

    def did(self, ins, tally=None):
        tally = tally or self.steps
        ins.then_inc(tally.sem, 1)
        tally.n += 1
        self.last = (tally.sem, tally.n)

    def settled(self):
        if self.last:
            self.eng.wait_ge(*self.last)

    def tell(self, tally):
        self.settled()
        self.eng.sem_inc(tally.sem, 1)
        tally.n += 1


ARENA = 76
Z_, GA_, GB_ = 0, 14, 22
QK_, KZ_, KI_ = 30, 39, 43
ISC_, REL_, MB_, SC_, PT_, VT_, OS_ = 47, 48, 52, 54, 58, 62, 63
RAW_, DIF_ = 65, 71
CS_, CONV_, CU_ = 65, 66, 70
XN_, SQ_, STD_, RSTD_ = 58, 66, 74, 75
SW_, L_, PD_, PI_, PV_, A_, KK_, G_, BON_, TMP_, TL_, SG_, RESET_ = 30, 34, 38, 42, 46, 50, 54, 58, 62, 66, 70, 71, 72
GM_, GN_, VTOK_ = 30, 66, 38
NB_, UD_, TD_, YT_ = 42, 8, 54, 54
Q2A_, Q2B_, BD_, PROD_, UT_ = 12, 74, 12, 13, 74
S_, RHS_, SA_, STMP_ = 12, 13, 74, 75
YC_, YSQ_ = 30, 34
CV_, SIL_, HID_ = 30, 34, 36
BV_, BO_, BZ_, BG_, BX_, BKZ_ = (0, 56), 8, (16, 40), (24, 48), 32, 36
BTMP_, BSC_, BPT_, BRAW_, BSQ_, BY_ = 64, 66, (72, 52), 40, 0, (48, 32)


def slots(buf, at, n=1):
    return buf[:, at * T:(at + n) * T].rearrange("p (n t) -> p n t", t=T)


def over(ap, n):
    return ap.unsqueeze(1).broadcast_to([ap.shape[0], n, ap.shape[1]])


class Core:

    def __init__(self, nc, ctx, dram, out):
        self.nc, self.dram, self.out = nc, dram, out

        def sb(name, shape, dt=F32):
            return ctx.enter_context(nc.sbuf_tensor(name, shape, dt))

        self.h = sb("residual", [P, KD, T])
        self.xh = sb("act_high", [P, 16, T], F32R)
        self.xl = sb("act_low", [P, 16, T], F32R)
        self.slab = [sb(f"slab{i}", [P, 2048]) for i in range(SLABS)]
        self.wh = [sb(f"w_high{i}", [P, 2048], F32R) for i in range(PARTS)]
        self.wl = [sb(f"w_low{i}", [P, 2048], F32R) for i in range(PARTS)]
        self.cc = sb("constants", [P, NCC])
        self.cm = sb("model_constants", [P, max(NCA, NCB)])
        self.rope = sb("rope", [P, 4, T])
        self.vec = sb("vectors", [P, max(NVA, NVB)])
        self.lora = sb("lora_weights", [P, 1024])
        self.ar = sb("arena", [P, ARENA * T])
        self.small = sb("small", [P, 192])
        self.gate = [ctx.enter_context(nc.semaphore(n)) for n in ("arrived", "left", "spare")]
        self.early = ctx.enter_context(nc.semaphore("early_slabs"))
        self.bank = [ctx.enter_context(nc.psum_tensor(f"bank{i}", [P, 512], F32)) for i in range(8)]
        self.d_blocks = nc.dram_tensor("d_blocks", (8, 16, SUB, SUB), F32, kind="Internal").ap()
        self.d_inverse = nc.dram_tensor("d_inverse", (P, 2, T), F32, kind="Internal").ap()
        self.sems = {}
        self.ctx = ctx

    def sem(self, name):
        if name not in self.sems:
            self.sems[name] = Tally(self.ctx.enter_context(self.nc.semaphore(name)))
        return self.sems[name]

    def fresh(self):
        for t in self.sems.values():
            t.restart()

    def const(self, name, n=P, table=None):
        table = table or CC
        buf = self.cc if table is CC else self.cm
        return buf[:, table[name]:table[name] + n]

    def causal(self, m):
        return self.const("causal", T)[:, P * (1 - m):T]

    def a(self, at, n=1):
        return slots(self.ar, at, n)


SLABS, PARTS = 3, 3
GEMM_BANKS = 3


def plan(units):
    rows, product, fill, freed = [], 0, 0, {}
    for kind, i in units:
        fills = 2 if kind.startswith("br") else 0 if kind == "down" else 1
        reader = "act" if kind in ("q", "kv", "qi", "ki", "rz", "ga", "gb", "gc", "z", "Z", "g", "G", "v", "V", "qk", "QK") else "dve"
        banks = []
        for _ in range(fills):
            b = fill % GEMM_BANKS
            fill += 1
            freed[b, reader] = freed.get((b, reader), 0) + 1
            banks.append((b, reader, freed[b, reader]))
        first = product
        product += max(fills, 1)
        rows.append((kind, i, first, product, banks))
    return rows


PLAN_A, PLAN_B = plan(UNITS_A), plan(UNITS_B)
PHASES = {"start": 0, "a": 1, "middle": 1 + LAYERS, "b": 2 + LAYERS}


def meet(core, line, phase, clears=False):
    line.settled()
    arrived, left, spare = core.gate
    eng = line.eng
    eng.sem_inc(arrived, 1)
    eng.wait_ge(arrived, phase * 5 + 5)
    eng.sem_inc(spare, 1)
    if clears:
        numbers = sorted(t.sem.num for t in core.sems.values())
        assert numbers[-1] - numbers[0] == len(numbers) - 1
        eng.sem_clear(range(numbers[0], numbers[-1] + 1))
    eng.sem_inc(left, 1)
    eng.wait_ge(left, phase * 5 + 5)
    eng.sem_inc(spare, 1)
    line.last = None


ROUND_NEXT = ("round", None)


def woven(units, lead, after):
    steps, rounded = lead[:4], 0
    for u in range(1 - PARTS, len(units)):
        ahead = u + PARTS - 1
        if ahead < len(units):
            if rounded == ahead:
                steps.append(("round", ahead))
                rounded += 1
            steps.append(("split", ahead))
        if u < 0:
            continue
        if u == 0:
            third = steps[-2:]
            steps = steps[:-2] + lead[4:] + third
        steps.append(("unit", u))
        for step in after.get(units[u], []):
            if step == ROUND_NEXT:
                if rounded < len(units):
                    steps.append(("round", rounded))
                    rounded += 1
            else:
                steps.append(step)
    return steps


def schedule_a():
    after = {}

    def put(unit, *steps):
        after.setdefault(unit, []).extend(steps)

    put(("kv", 0), ("rope", 0), ("rope", 1))
    put(("qi", 0), ("rope", 2), ("v_tok", 0))
    put(("ki", 0), ("w_idx", 0), ("rope", 3), ("k_pad", 0))
    put(("rz", 0), ("rope", 4), ("k_pad", 1))
    put(("rz", 1), ("ki_pad", 0), ("isc", 0), ("isc", 1))
    put(("rz", 2), ("isc", 2), ("isc", 3), ("topk", 0), ("topk", 1))
    put(("rz", 3), ("isc", 4), ("isc", 5))
    put(("rz", 4), ("isc", 6), ("isc", 7), ("topk", 2))
    put(("rz", 5), ("topk", 3))
    hosts = [("rz", 6)] + [("uc", i) for i in range(4)] + [("cb", i) for i in range(2)] + [("ga", i) for i in range(4)]
    for i, unit in enumerate(hosts):
        put(unit, ROUND_NEXT, *[(name, i - lag) for name, lag in (("scores", 0), ("turn", 1), ("pv", 2)) if 0 <= i - lag < 8])
        if i == 9:
            put(unit, ("lora_inputs", 0))
        if i in (5, 9):
            put(unit, ("divide", (i - 5) // 4))
        if i in (6, 10):
            put(unit, ("attn_out", (i - 6) // 4))
    for i in range(4):
        put(("uc", i), ("conv", i))
    put(("ga", 3), ("lora", 0), ("gate", 0))
    put(("gb", 0), ("decay", 0))
    put(("gb", 1), ROUND_NEXT, ("k_norm", 0))
    put(("gb", 2), ("k_norm", 1), ROUND_NEXT, ("keys", 0))
    put(("gb", 3), ("gate", 1))
    put(("br0", 0), ("chunk", 0), ("keys", 1), ("mask", 0), ("chunk", 1), ("mask", 1))
    put(("br0", 1), ("chunk", 2), ("mask", 2), ("chunk", 3), ("mask", 3), ("blocks_out", 0), ("tok", 0), ("tok", 1), ("tok", 2), ("invert", 0))
    put(("br1", 0), ("blocks_turn", 0), ("off_diag", 0))
    put(("br1", 1), ("inverses_out", 0))
    put(("gc", 0), ("blocks_in", 0))
    put(("gc", 1), ("solve", 0))
    put(("gc", 2), ("solve", 1), ("solve", 2), ("solve", 3))
    for c in range(NCH):
        put(("gc", 2 if c < 2 else 3), ("scan_rhs", c), ("scan_sa", c), ("scan_y", c))
    put(("gc", 3), ("gn", 0), ("gn", 1), ("gate", 2))
    for i in range(4):
        put(("out", min(i + 1, 3)), ("square", i))
    put(("out", 3), ("norm", 1))
    put(("up", FT - 1), ("ffn", FT), ("ffn", FT + 1))
    lead = [("square", i) for i in range(4)] + [("params", 0), ("norm", 0)]
    return woven(UNITS_A, lead, after)


def schedule_b():
    after = {}

    def put(unit, *steps):
        after.setdefault(unit, []).extend(steps)

    for kind, (v, qk, z) in enumerate((("v", "qk", "z"), ("V", "QK", "Z"))):
        hosts = [(v, 1), (v, 2), (v, 3), (qk, 0)]
        for i in range(4):
            put(hosts[i], ("v_turn", 4 * kind + i))
            if kind:
                put(hosts[i], ("post", i))
        hosts = [(qk, n) for n in range(8)] + [(z, n) for n in range(4)]
        for n in range(1, 12):
            flow = (("swap", 1), ("turn", 4), ("scores", 2), ("pv", 4))
            steps = [(name, 8 * kind + n - lag) for name, lag in flow if 0 <= n - lag < 8]
            at = [name == "scores" for name, _ in steps].index(True) if n in range(2, 10) else len(steps)
            put(hosts[n], *steps[:at], ROUND_NEXT, *steps[at:])
    put(("z", 3), ("silu", 0))
    put(("g", 0), ("rms", 0))
    put(("g", 1), ("silu", 1))
    put(("G", 0), ("gate", 0))
    put(("pa", 0), ("gate", 1))
    for i in range(4):
        put(("pa", i), ("post", 4 + i))
    lead = [("square", i) for i in range(4)] + [("params", 0), ("norm", 0), ("lam", 0)]
    return woven(UNITS_B, lead, after)


SCHED_A, SCHED_B = schedule_a(), schedule_b()


def first_slabs(core, eng, slabs, layer):
    for u in range(SLABS):
        eng.dma_start(core.slab[u][:], slabs[layer, u]).then_inc(core.early, 16)


def stream(core, eng, slabs, layer):
    count = slabs.shape[1]
    flat_slabs = slabs.rearrange("l u p n -> (l u) p n")
    split = core.sem("slab_split")
    whole = (count - SLABS) // SLABS
    with eng.Fori(0, whole) as r:
        for s in range(SLABS):
            eng.wait_ge(split.sem, r * SLABS + (s + 1))
            eng.dma_start(core.slab[s][:], flat_slabs[layer * count + r * SLABS + (SLABS + s)]).then_inc(
                core.sem(f"slab_in{s}").sem, 16)
    for u in range(SLABS * (whole + 1), count):
        eng.wait_ge(split.sem, u - SLABS + 1)
        eng.dma_start(core.slab[u % SLABS][:], flat_slabs[layer * count + u]).then_inc(
            core.sem(f"slab_in{u % SLABS}").sem, 16)
    for s in range(SLABS):
        eng.wait_ge(core.sem(f"slab_in{s}").sem, 16 * (len(range(s, count, SLABS)) - 1))
    eng.wait_ge(split.sem, count)


def slab_in(core, eng, u, earlier):
    if u >= SLABS:
        eng.wait_ge(core.sem(f"slab_in{u % SLABS}").sem, 16 * (u // SLABS))
    elif u == 0:
        eng.wait_ge(core.early, earlier * (16 * SLABS) + 16 * SLABS)
        eng.sem_inc(core.gate[2], 1)


def sync_program(core, eng):
    d, line = core.dram, Line(eng, core.sem("sync_steps"))
    eng.dma_start(flat(core, 6).bitcast(I32), d["positions"].to_broadcast([P, T])).then_inc(core.sem("pos_in").sem, 16)
    eng.dma_start(core.cm[:, 0:NCA], d["const_a"]).then_inc(core.sem("model_in").sem, 16)
    eng.dma_start(core.h[:], d["x_t"]).then_inc(core.sem("x_in").sem, 16)
    eng.dma_start(core.cc[:], d["common"]).then_inc(core.sem("const_in").sem, 16)
    first_slabs(core, eng, d["stream_a"], 0)
    for name in ("x_in", "const_in", "model_in", "pos_in"):
        eng.wait_ge(core.sem(name).sem, 16)
    meet(core, line, PHASES["start"])

    def layer_a(layer, following, index):
        eng.dma_start(core.vec[:, 0:NVA], d["vec_a"][layer]).then_inc(core.sem("vec_in").sem, 16)
        eng.dma_start(core.lora[:], d["lora"][layer]).then_inc(core.sem("lora_in").sem, 16)
        stream(core, eng, d["stream_a"], layer)
        eng.wait_ge(core.sem("vec_in").sem, 16)
        eng.wait_ge(core.sem("lora_in").sem, 16)
        first_slabs(core, eng, following, index)
        meet(core, line, layer + PHASES["a"])

    def layer_b(layer, more):
        eng.dma_start(core.vec[:, 0:NVB], d["vec_b"][layer]).then_inc(core.sem("vec_in").sem, 16)
        stream(core, eng, d["stream_b"], layer)
        eng.wait_ge(core.sem("vec_in").sem, 16)
        if more:
            first_slabs(core, eng, d["stream_b"], layer + 1)
        meet(core, line, layer + PHASES["b"])

    if core.layers_a > 1:
        with eng.Fori(0, core.layers_a - 1) as layer:
            layer_a(layer, d["stream_a"], layer + 1)
    layer_a(core.layers_a - 1, d["stream_b"], 0)
    eng.dma_start(core.cm[:, 0:NCB], d["const_b"]).then_inc(core.sem("model_in").sem, 16)
    eng.wait_ge(core.sem("model_in").sem, 16)
    meet(core, line, PHASES["middle"])
    if core.layers_b > 1:
        with eng.Fori(0, core.layers_b - 1) as layer:
            layer_b(layer, True)
    layer_b(core.layers_b - 1, False)
    core.fresh()
    core.sem("final_norm").take(eng, 8)
    eng.dma_start(core.out, core.h[:]).then_inc(core.sem("out_done").sem, 16)
    eng.wait_ge(core.sem("out_done").sem, 16)


def emptied(core, eng, rows, u):
    for bank, reader, n in rows[u][4]:
        eng.wait_ge(core.sem(f"{reader}_emptied{bank}").sem, n)


def made(core, eng, rows, u, part=0):
    eng.wait_ge(core.sem("products").sem, rows[u][2] + part + 1)


def walk(schedule, does):
    for name, i in schedule:
        if name in does:
            does[name](i)


def act_round(core, line, rows, earlier):
    eng = line.eng

    def step(u):
        slab_in(core, eng, u, earlier)
        if u >= PARTS:
            eng.wait_ge(core.sem("products").sem, rows[u - PARTS][3])
        line.did(eng.activation(core.wh[u % PARTS][:], core.slab[u % SLABS][:], ACT.Copy), core.sem("slab_high"))

    return step


def act_norm(core, line, split_out):
    eng = line.eng

    def square(i):
        line.did(eng.activation(core.a(SQ_ + 2 * i, 2), core.h[:, 2 * i:2 * i + 2, :], ACT.Square), core.sem("squared"))

    def norm(_):
        core.sem("mean_square").take(eng)
        line.did(eng.activation(core.a(STD_)[:, 0], core.bank[7][:, 0:T], ACT.Sqrt, bias=core.small[:, 0:1],
                                scale=1.0 / D), core.sem("act_emptied7"))
        if split_out:
            for i in range(4):
                core.sem("normed").take(eng)
                line.did(eng.activation(core.xh[:, 2 * i:2 * i + 2, :], core.a(XN_ + 2 * i, 2), ACT.Copy),
                         core.sem("x_high"))

    return square, norm


UA = {unit: u for u, unit in enumerate(UNITS_A)}
UB = {unit: u for u, unit in enumerate(UNITS_B)}
WIDTH = {0: P, 1: T}


def heads(ap, width):
    return ap[:, 0:2 * width].rearrange("p (h s) -> p h s", h=2)


def flat(core, at, n=1):
    return core.ar[:, at * T:(at + n) * T]


def raw_tile(core):
    return core.ar[:, RAW_ * T:RAW_ * T + 4 * (T + 1)].rearrange("p (r j t) -> p r j t", r=2, j=2)


def scalar_a(core, eng, line, layer):
    rows, sem, bank, vec = PLAN_A, core.sem, core.bank, core.vec
    round_slab, (square0, norm0) = act_round(core, line, rows, layer), act_norm(core, line, True)

    def act(out, in_, func, tally=None, **kw):
        line.did(eng.activation(out, in_, func, **kw), tally)

    def square(i):
        if square.later:
            sem("residual_done").take(eng)
        square0(i)
        if i == 3:
            square.later = True
    square.later = False

    def ffn(j):
        if j < FT:
            made(core, eng, rows, UA["up", j])
            if j >= 2:
                sem("hidden").at_least(eng, j - 1)
            for half in range(2):
                act(core.a(CV_ + 2 * (j % 2) + half)[:, 0], bank[rows[UA["up", j]][4][0][0]][:, half * T:half * T + T],
                    ACT.Identity, sem("newest_tap") if half else None,
                    scale=vec[:, VA["conv"] + 4 * FT + half * FT + j:][:, 0:1])
        if 1 <= j <= FT:
            sem("convolved").take(eng)
            act(core.a(SIL_ + (j - 1) % 2)[:, 0], core.a(CV_ + 2 * ((j - 1) % 2))[:, 0], ACT.Silu, sem("silu"))
        if j >= 2:
            sem("hidden").take(eng)
            if j - 2 >= 8:
                eng.wait_ge(sem("products").sem, rows[UA["down", (j - 10) // 2]][3])
            act(core.xh[:, 8 + (j - 2) % 8, :], core.a(HID_ + (j - 2) % 4)[:, 0], ACT.Copy, sem("hidden_high"))

    def unit(u):
        kind, i, _, _, banks = rows[u]
        if kind in ("q", "kv", "qi", "ki"):
            made(core, eng, rows, u)
            at = {"q": 2 * i, "kv": 4, "qi": 6, "ki": 8}[kind]
            n = 1 if kind == "ki" else 2
            act(flat(core, QK_ + at, n), bank[banks[0][0]][:, 0:n * T], ACT.Copy, sem(f"act_emptied{banks[0][0]}"))
        elif kind == "rz":
            made(core, eng, rows, u)
            sem("z_mixed").at_least(eng, i - 1)
            act(raw_tile(core)[:, i % 2, :, 1:T + 1], heads(bank[banks[0][0]], T), ACT.Copy,
                sem(f"act_emptied{banks[0][0]}"))
        elif kind == "uc":
            made(core, eng, rows, u)
            if i:
                emptied(core, eng, rows, u - 1)
            else:
                sem("z_mixed").at_least(eng, 7)
            act(flat(core, CS_), bank[banks[0][0]][:, T:2 * T], ACT.Copy, sem("c_copied"))
        elif kind == "cb":
            emptied(core, eng, rows, u)
            act(core.xh[:, 12 + 2 * i:14 + 2 * i, :], core.a(CONV_ + 2 * i, 2), ACT.Copy, sem("yb_high"))
        elif kind in ("ga", "gb", "gc"):
            made(core, eng, rows, u)
            g = "abc".index(kind[1])
            if kind == "gc":
                sem("summed").at_least(eng, 4)
            for k in range(2):
                act(flat(core, (GA_ if g == 0 else GB_) + 2 * i + k), bank[banks[0][0]][:, k * T:k * T + T],
                    ACT.Identity, sem(f"act_emptied{banks[0][0]}") if k else None,
                    bias=vec[:, VA["b_gate"] + 8 * g + 2 * i + k:][:, 0:1])
        elif kind == "br2":
            for k in range(2):
                eng.wait_ge(sem("summed").sem, 4 + 2 * i + k + 1)
                act(core.xh[:, 4 + 4 * i + 2 * k:][:, 0:2, :], core.a(GA_ + 4 * i + 2 * k, 2), ACT.Copy, sem("mix_high"))
        elif kind == "up":
            ffn(i)

    def gate(g):
        line.settled()
        act(flat(core, GA_ if g == 0 else GB_, 8), flat(core, GA_ if g == 0 else GB_, 8), ACT.Sigmoid, sem("gated"))

    def k_pad(n):
        sem("k_padded").take(eng)
        act(flat(core, KZ_ + 2 * n, 2), bank[3 + n][:], ACT.Copy, sem(f"act_emptied{3 + n}"))

    def ki_pad(_):
        for n in range(2):
            sem("ki_padded").take(eng)
            act(flat(core, KI_ + 2 * n, 2), bank[5 + n][:], ACT.Copy, sem(f"act_emptied{5 + n}"))

    def v_tok(_):
        sem("v_turned").take(eng)
        act(flat(core, VT_), bank[7][:, 0:T], ACT.Copy, sem("act_emptied7"))

    def isc(k):
        width = WIDTH[k // 4]
        sem("index_scores").take(eng)
        if k >= 2:
            sem("index_summed").at_least(eng, k - 1)
        act(heads(flat(core, REL_ + 2 * (k % 2), 2), width), heads(bank[3 + k % 2], width), ACT.Relu,
            sem(f"act_emptied{3 + k % 2}"))

    def scores(k):
        width = WIDTH[k // 4]
        sem("maxed").take(eng)
        buf = heads(flat(core, SC_ + 2 * (k % 2), 2), width)
        for p in range(2):
            act(buf[:, p, :], buf[:, p, :], ACT.Exp, sem("exps") if p else None, bias=core.small[:, 8 + 2 * (k % 2) + p:][:, 0:1],
                accum_out=core.small[:, 16 + 2 * k + p:][:, 0:1])

    def turn(k):
        n = 2 * (k // 4 + 1) * P
        sem("turned").take(eng)
        if k >= 2:
            sem("weighted").at_least(eng, k - 1)
        act(flat(core, PT_ + 2 * (k % 2), 2)[:, 0:n], bank[7][:, 0:n], ACT.Copy, sem("act_emptied7"))

    def attn_out(m):
        sem("outputs_turned").take(eng)
        act(core.xh[:, 8:12, m * P:m * P + P], bank[7][:].rearrange("p (j t) -> p j t", j=4), ACT.Copy, sem("ya_high"))

    def lora_inputs(_):
        sem("z_mixed").at_least(eng, 7)
        act(flat(core, TL_)[0:64, :], flat(core, Z_ + 12)[0:64, :], ACT.Tanh)
        act(flat(core, SG_), flat(core, Z_ + 13), ACT.Sigmoid, sem("lora_inputs"))

    def lora(_):
        for half, at, base in ((0, SW_, "w0"), (1, A_, "a0")):
            for b in range(2):
                sem("lora_made").take(eng)
                for k in range(2):
                    j, src = 2 * b + k, 3 + 2 * half + b
                    act(flat(core, at + j), bank[src][:, k * T:k * T + T], ACT.Sigmoid,
                        sem(f"act_emptied{src}") if k else None, bias=vec[:, VA[base] + j:][:, 0:1])
        for b, src in ((0, 7), (1, 3)):
            sem("lora_made").take(eng)
            act(flat(core, G_ + 2 * b, 2), bank[src][:], ACT.Copy, sem(f"act_emptied{src}"))

    def decay(_):
        sem("summed_decay").take(eng)
        act(flat(core, PD_, 4), flat(core, L_, 4), ACT.Exp, scale=-DECAY)
        act(flat(core, PI_, 4), flat(core, L_, 4), ACT.Exp, scale=DECAY)
        sem("summed_decay").take(eng)
        act(flat(core, PV_, 4), flat(core, SW_, 4), ACT.Exp, sem("decays"), scale=-DECAY)

    def k_norm(part):
        if part == 0:
            sem("kk").take(eng)
            act(flat(core, TMP_, 4), flat(core, KK_, 4), ACT.Square, sem("kk_squared"))
            sem("clamped").take(eng)
            act(flat(core, SG_)[0:8, :], flat(core, TL_)[0:8, :], ACT.Sqrt, sem("rooted"))

    def tok(x):
        dst = (VTOK_, Z_, Z_ + 4)[x]
        for b in range(2):
            sem("tok_made").take(eng)
            act(flat(core, dst + 2 * b, 2), bank[(7, 3)[b]][:], ACT.Copy, sem(f"act_emptied{(7, 3)[b]}"))

    def blocks_out(_):
        sem("masked").take(eng)
        g = flat(core, GM_, 8).rearrange("p (cj a t) -> p cj a t", cj=16, a=2)
        for n in range(8):
            q = n % 4
            eng.dma_start(core.d_blocks[n].rearrange("c i t -> i c t"), g[SUB * n:SUB * n + SUB, :, 0, SUB * q:SUB * q + SUB]).then_inc(
                sem("blocks_written").sem, 16)

    def blocks_turn(_):
        eng.wait_ge(sem("blocks_written").sem, 16 * 8)
        eng.dma_start(flat(core, BD_), core.d_blocks.rearrange("n c i t -> (n c) (i t)")).then_inc(
            sem("blocks_in").sem, 16)

    def inverses_out(_):
        sem("inverted").take(eng)
        eng.dma_start(core.d_inverse, flat(core, UT_, 2).rearrange("p (w n) -> p w n", w=2)).then_inc(
            sem("inverses_written").sem, 16)

    def blocks_in(_):
        sem("inverses_written").take(eng, 16)
        sem("off_diagonal").take(eng)
        for n in range(8):
            q = n % 4
            for way, dst in ((0, UD_), (1, TD_)):
                to = flat(core, dst, 4).rearrange("p (cj t) -> p cj t", cj=16)
                eng.dma_start(to[SUB * n:SUB * n + SUB, :, SUB * q:SUB * q + SUB],
                              core.d_inverse[SUB * n:SUB * n + SUB, way, :].rearrange("cj (i t) -> i cj t", i=SUB)
                              ).then_inc(sem("inverses_in").sem, 16)

    def solve(s):
        if s == 0:
            for b in range(2):
                sem("solved").take(eng)
                act(flat(core, (Q2A_, Q2B_)[b], 2), bank[3 + b][:], ACT.Copy, sem(f"act_emptied{3 + b}"))

    def scan_rhs(c):
        sem("rhs_made").take(eng)
        act(flat(core, RHS_), bank[3][:, 0:T], ACT.Copy, sem("act_emptied3"))

    def scan_sa(c):
        sem("sa_made").take(eng)
        act(flat(core, SA_), bank[4][:, 0:T], ACT.Copy, sem("act_emptied4"))

    def scan_y(c):
        sem("y_made").take(eng)
        act(core.a(YT_, 4)[:, :, c * CH:c * CH + CH], bank[6][:, 0:T].rearrange("p (j t) -> p j t", j=4), ACT.Copy,
            sem("act_emptied6"))

    def gn(part):
        if part == 0:
            sem("centred").take(eng)
            act(flat(core, YSQ_, 4), flat(core, YC_, 4), ACT.Square, sem("y_squared"))
            sem("y_variance").take(eng)
            act(flat(core, TL_)[0:8, :], bank[5][0:8, 0:T], ACT.Sqrt, sem("act_emptied5"), bias=core.small[0:8, 1:2],
                scale=1.0 / HD)
        else:
            sem("yc").take(eng)
            made(core, eng, rows, UA["gc", 3])
            act(core.xh[:, 0:4, :], core.a(YC_, 4), ACT.Copy, sem("yc_high"))

    walk(SCHED_A, dict(params=lambda _: eng.wait_ge(sem("vec_in").sem, 16), round=round_slab, square=square, norm=norm0, unit=unit, gate=gate, k_pad=k_pad, ki_pad=ki_pad, v_tok=v_tok,
                       isc=isc, scores=scores, turn=turn, attn_out=attn_out, lora_inputs=lora_inputs, lora=lora, decay=decay, k_norm=k_norm,
                       tok=tok, blocks_out=blocks_out, blocks_turn=blocks_turn, inverses_out=inverses_out, blocks_in=blocks_in, solve=solve, scan_rhs=scan_rhs,
                       scan_sa=scan_sa, scan_y=scan_y, gn=gn, ffn=ffn))
    eng.wait_ge(sem("inverses_in").sem, 16 * 16)


def scalar_program(core, eng):
    line, sem = Line(eng, core.sem("act_steps")), core.sem
    square, norm = act_norm(core, line, False)
    for r in range(2):
        sem("angles").take(eng)
        for k in range(2):
            line.did(eng.activation(core.rope[:, 2 * r + k, :], core.a(2 * r + k)[:, 0], ACT.Sin))
    meet(core, line, PHASES["start"])
    core.fresh()
    with eng.Fori(0, core.layers_a) as layer:
        scalar_a(core, eng, line, layer)
        meet(core, line, layer + PHASES["a"])
    core.fresh()
    for i in range(4):
        square(i)
    norm(0)
    meet(core, line, PHASES["middle"])
    core.fresh()
    with eng.Fori(0, core.layers_b) as layer:
        scalar_b(core, eng, line, layer + core.layers_a)
        meet(core, line, layer + PHASES["b"])
    core.fresh()
    for i in range(4):
        square(i)
    norm(0)


EPS_, GNEPS_, SUBEPS_, LAM_, NMAX_, DEN_, WI_, TOP_, PC_, RDEN_ = 0, 1, 2, 4, 8, 16, 80, 96, 104, 120


def dve_split(core, line):
    def step(u):
        line.eng.wait_ge(core.sem("slab_high").sem, u + 1)
        line.did(line.eng.tensor_tensor(core.wl[u % PARTS][:], core.slab[u % SLABS][:],
                                        core.wh[u % PARTS][:].bitcast(F32), ALU.subtract), core.sem("slab_split"))

    return step


def dve_norm(core, line, gain, split_out, root_uses):
    eng, sem = line.eng, core.sem

    def step(_):
        eng.wait_ge(sem("act_emptied7").sem, root_uses)
        line.did(eng.reciprocal(flat(core, RSTD_), flat(core, STD_)))
        line.settled()
        for k in range(KD):
            out = core.a(XN_ + k)[:, 0] if split_out else core.h[:, k, :]
            done = sem("final_norm") if not split_out else sem("normed") if k % 2 else None
            line.did(eng.scalar_tensor_tensor(out=out, in0=core.h[:, k, :], scalar=gain(k), in1=flat(core, RSTD_),
                                              op0=ALU.mult, op1=ALU.mult), done)
        if split_out:
            for i in range(4):
                sem("x_high").take(eng)
                line.did(eng.tensor_tensor(core.xl[:, 2 * i:2 * i + 2, :], core.a(XN_ + 2 * i, 2),
                                           core.xh[:, 2 * i:2 * i + 2, :].bitcast(F32), ALU.subtract), sem("x_ready"))

    return step


def vector_a(core, eng, line):
    rows, sem, bank, vec, did = PLAN_A, core.sem, core.bank, core.vec, line.did
    split = dve_split(core, line)
    tt, ts, stt = eng.tensor_tensor, eng.tensor_scalar, eng.scalar_tensor_tensor

    def col(name, j):
        return vec[:, VA[name] + j:][:, 0:1]

    def norm(which):
        dve_norm(core, line, lambda k: col(("norm", "ffn_norm")[which], k), True, (1, FFN_NORM_USE_OF_7)[which])(0)

    def low(dst_at, n, src, high, ready):
        sem(high).take(eng)
        d = core.xl[:, dst_at:dst_at + n, :]
        hi = core.xh[:, dst_at:dst_at + n, :]
        did(tt(d, src, hi.bitcast(F32), ALU.subtract), sem(ready))

    def ffn(j):
        if j < FT:
            sem("newest_tap").take(eng)
            b = rows[UA["up", j]][4][0][0]
            for half in range(2):
                out, src = core.a(CV_ + 2 * (j % 2) + half)[:, 0], bank[b][:, half * T:half * T + T]
                for tap in (1, 0):
                    lag = 2 - tap
                    if lag == 2:
                        line.settled()
                    did(stt(out=out[:, lag:T], in0=src[:, 0:T - lag],
                            scalar=col("conv", 2 * FT * tap + half * FT + j), in1=out[:, lag:T], op0=ALU.mult,
                            op1=ALU.add), sem(f"dve_emptied{b}") if half and lag == 2 else None)
            line.tell(sem("convolved"))
        if 1 <= j <= FT:
            i = j - 1
            sem("silu").take(eng)
            if i >= 4:
                sem("hidden_high").at_least(eng, i - 3)
                line.settled()
            did(tt(flat(core, HID_ + i % 4), flat(core, SIL_ + i % 2), flat(core, CV_ + 2 * (i % 2) + 1), ALU.mult),
                sem("hidden"))
        if j >= 2:
            i = j - 2
            low(8 + i % 8, 1, core.a(HID_ + i % 4), "hidden_high", "hidden_low")

    def unit(u):
        kind, i, _, _, banks = rows[u]
        if kind == "rz":
            if i == 0:
                line.settled()
                did(eng.memset(raw_tile(core)[:, :, :, 0:1], 0.0))
            emptied(core, eng, rows, u)
            raw = raw_tile(core)[:, i % 2]
            line.settled()
            did(tt(core.a(DIF_, 2), raw[:, :, 0:T], raw[:, :, 1:T + 1], ALU.subtract))
            line.settled()
            for k in range(2):
                did(stt(out=flat(core, Z_ + 2 * i + k), in0=flat(core, DIF_ + k), scalar=col("mu", 2 * i + k),
                        in1=raw[:, k, 1:T + 1], op0=ALU.mult, op1=ALU.add), sem("z_mixed") if k else None)
            if i == 6:
                line.settled()
                did(eng.memset(cu_tile(core)[:, :, 0:2], 0.0))
        elif kind == "uc":
            sem("c_copied").take(eng)
            did(tt(cu_tile(core)[:, i, 2:T + 2], bank[banks[0][0]][:, 0:T], flat(core, CS_), ALU.mult),
                sem(f"dve_emptied{banks[0][0]}"))
        elif kind == "cb":
            made(core, eng, rows, u)
            line.settled()
            did(tt(flat(core, CONV_ + 2 * i, 2), bank[banks[0][0]][:], flat(core, CONV_ + 2 * i, 2), ALU.mult),
                sem(f"dve_emptied{banks[0][0]}"))
            low(12 + 2 * i, 2, core.a(CONV_ + 2 * i, 2), "yb_high", "yb_ready")
        elif kind in ("br0", "br1", "br2"):
            g = int(kind[2])
            for k in range(2):
                at = 4 * i + 2 * k
                src = flat(core, (GA_ if g == 0 else GB_) + at, 2)
                if i == 0 and k == 0:
                    sem("gated").take(eng)
                made(core, eng, rows, u, k)
                did(tt(src, bank[banks[k][0]][:], src, ALU.mult), sem(f"dve_emptied{banks[k][0]}"))
                if g:
                    line.settled()
                    did(tt(flat(core, GA_ + at, 2), flat(core, GA_ + at, 2), src, ALU.add), sem("summed"))
            if g == 2:
                for k in range(2):
                    low(4 + 4 * i + 2 * k, 2, core.a(GA_ + 4 * i + 2 * k, 2), "mix_high", "mix_ready")
        elif kind == "out":
            made(core, eng, rows, u)
            res = core.h[:, 2 * i:2 * i + 2, :]
            did(tt(res, heads(bank[banks[0][0]], T), res, ALU.add), sem(f"dve_emptied{banks[0][0]}"))
            line.tell(core.sem("residual_done"))
        elif kind == "up":
            ffn(i)
        elif (kind, i) == ("down", FT // 2 - 1):
            made(core, eng, rows, u)
            for b in range(4):
                res = core.h[:, 2 * b:2 * b + 2, :]
                did(tt(res, heads(bank[3 + b], T), res, ALU.add), sem(f"dve_emptied{3 + b}"))

    def conv(j):
        line.settled()
        out, src = flat(core, CONV_ + j), cu_tile(core)[:, j]
        did(ts(out, src[:, 2:T + 2], col("sc", 8 + j), None, ALU.mult))
        line.settled()
        did(stt(out=out, in0=src[:, 1:T + 1], scalar=col("sc", 4 + j), in1=out, op0=ALU.mult, op1=ALU.add))
        line.settled()
        did(stt(out=out, in0=src[:, 0:T], scalar=col("sc", j), in1=out, op0=ALU.mult, op1=ALU.add))

    def rope(r):
        at, n, b, table = ((0, 2, 3, 0), (2, 2, 4, 0), (4, 1, 5, 0), (6, 2, 6, 2), (8, 1, 7, 2))[r]
        tmp = core.a(PT_ + 2 * (r % 2), n)
        sem("swapped").take(eng)
        did(tt(tmp, bank[b][:, 0:n * T].rearrange("p (n t) -> p n t", n=n), over(core.rope[:, table + 1, :], n), ALU.mult),
            sem(f"dve_emptied{b}"))
        did(tt(core.a(QK_ + at, n), core.a(QK_ + at, n), over(core.rope[:, table, :], n), ALU.mult))
        line.settled()
        did(tt(core.a(QK_ + at, n), core.a(QK_ + at, n), tmp, ALU.add), sem("rotated"))

    def w_idx(_):
        sem("w_turned").take(eng)
        did(ts(core.small[:, WI_:WI_ + 16].rearrange("p (m h) -> p m h", m=2),
               bank[7][:, 0:T].rearrange("p (m c) -> p m c", m=2)[:, :, 32:40],
               float(IDX_HEADS ** -0.5 * IDX_DIM ** -0.5), None, ALU.mult), sem("dve_emptied7"))

    def isc(k):
        m, pair = k // 4, k % 4
        width = WIDTH[m]
        total = flat(core, ISC_)[:, 0:width]
        eng.wait_ge(sem(f"act_emptied{3 + k % 2}").sem, ISC_USES[k])
        rel = heads(flat(core, REL_ + 2 * (k % 2), 2), width)
        for p in range(2):
            h = 2 * pair + p
            before = core.causal(m) if h == 0 else total
            line.settled()
            did(stt(out=total, in0=rel[:, p, :], scalar=core.small[:, WI_ + 8 * m + h:][:, 0:1], in1=before,
                    op0=ALU.mult, op1=ALU.add), sem("index_summed") if p else None)

    def topk(part):
        m, width = part // 2, WIDTH[part // 2]
        total, top = flat(core, ISC_)[:, 0:width], core.small[:, TOP_:TOP_ + 8]
        for _ in range(TOPK // 16):
            line.settled()
            did(eng.max(top, total))
            line.settled()
            did(eng.match_replace(total, top, total, TAKEN))
        if part % 2 == 0:
            return
        line.settled()
        did(ts(total, total, 0.9 * TAKEN, NEG, ALU.is_gt, ALU.mult))
        line.settled()
        did(tt(flat(core, MB_ + m)[:, 0:width], total, core.causal(m), ALU.add))

    def scores(k):
        m, width = k // 4, WIDTH[k // 4]
        sem("scored").take(eng)
        if k >= 2:
            eng.wait_ge(sem("turned").sem, k - 1)
        b = 5 + k % 2
        buf = heads(flat(core, SC_ + 2 * (k % 2), 2), width)
        line.settled()
        did(stt(out=buf, in0=heads(bank[b], width), scalar=HD ** -0.5, in1=over(flat(core, MB_ + m)[:, 0:width], 2),
                op0=ALU.mult, op1=ALU.add), sem(f"dve_emptied{b}"))
        line.settled()
        mx = core.small[:, NMAX_ + 2 * (k % 2):NMAX_ + 2 * (k % 2) + 2]
        did(eng.tensor_reduce(mx, buf, AX_X, ALU.max))
        line.settled()
        did(ts(mx, mx, -1.0, None, ALU.mult), sem("maxed"))

    def divide(m):
        sem("weighted").take(eng, 4)
        den, rden = core.small[:, DEN_ + 8 * m:][:, 0:8], core.small[:, RDEN_:RDEN_ + 8]
        if m:
            sem("outputs_turned").at_least(eng, 1)
        line.settled()
        did(eng.reciprocal(rden, den))
        line.settled()
        out = flat(core, OS_, 2).rearrange("p (h d) -> p h d", h=8)
        did(tt(out, bank[3 + m][:].rearrange("p (h d) -> p h d", h=8),
               rden.unsqueeze(2).broadcast_to([P, 8, HD]), ALU.mult), sem(f"dve_emptied{3 + m}"))
        line.settled()
        line.tell(core.sem("divided"))

    def attn_out(m):
        sem("ya_high").take(eng)
        did(tt(core.xl[:, 8:12, m * P:m * P + P], bank[7][:].rearrange("p (j t) -> p j t", j=4),
               core.xh[:, 8:12, m * P:m * P + P].bitcast(F32), ALU.subtract), sem("dve_emptied7"))
        line.tell(sem("ya_done"))

    def decay(_):
        line.settled()
        reset = flat(core, RESET_, 4)
        did(eng.memset(reset, 1.0))
        line.settled()
        did(eng.memset(reset.rearrange("p (c t) -> p c t", t=CH)[:, :, 0:1], 0.0))
        eng.wait_ge(sem("act_emptied3").sem, LORA_USES_OF_3)
        line.settled()
        did(eng.tensor_tensor_scan(flat(core, L_, 4), reset, flat(core, SW_, 4), 0.0, ALU.mult, ALU.add),
            sem("summed_decay"))
        line.settled()
        did(tt(flat(core, SW_, 4), flat(core, L_, 4), flat(core, SW_, 4), ALU.subtract), sem("summed_decay"))

    def k_norm(part):
        if part == 0:
            for j in range(4):
                did(ts(flat(core, KK_ + j), flat(core, Z_ + 4 + j), col("k_k", j), None, ALU.mult),
                    sem("kk") if j == 3 else None)
            sem("kk_summed").take(eng)
            did(ts(flat(core, TL_)[0:8, :], bank[5][0:8, 0:T], 1e-24, None, ALU.max), sem("dve_emptied5"))
            line.tell(core.sem("clamped"))
            sem("rooted").take(eng)
            did(eng.reciprocal(flat(core, TL_)[0:8, :], flat(core, SG_)[0:8, :]), sem("k_scale"))
        else:
            for b in range(2):
                sem("spread_made").take(eng)
                kk = flat(core, KK_ + 2 * b, 2)
                did(tt(kk, bank[6 + b][:], kk, ALU.mult), sem(f"dve_emptied{6 + b}"))

    def keys(part):
        a4, kk, zk, zr, tmp = (flat(core, x, 4) for x in (A_, KK_, Z_ + 4, Z_, TMP_))
        if part == 0:
            for j in range(4):
                did(ts(flat(core, TMP_ + j), flat(core, A_ + j), -1.0, col("k_a", j), ALU.add, ALU.mult))
            line.settled()
            did(stt(out=zk, in0=tmp, scalar=1.0, in1=zk, op0=ALU.add, op1=ALU.mult))
            line.settled()
            sem("decays").take(eng)
            did(stt(out=flat(core, PV_, 4), in0=kk, scalar=-1.0, in1=flat(core, PV_, 4), op0=ALU.mult, op1=ALU.mult))
            line.settled()
            did(tt(kk, kk, a4, ALU.mult))
            line.settled()
            did(tt(kk, kk, flat(core, PI_, 4), ALU.mult))
            did(eng.tensor_copy(core.small[:, PC_:PC_ + 16].rearrange("p (jc o) -> p jc o", o=1),
                                flat(core, PD_, 4).rearrange("p (jc t) -> p jc t", t=CH)[:, :, CH - 1:CH]))
            line.settled()
            did(tt(flat(core, PI_, 4), zk, flat(core, PI_, 4), ALU.mult))
            did(tt(a4, zr, flat(core, PD_, 4), ALU.mult), sem("keys_ready"))
            for j in range(4):
                did(stt(out=flat(core, TMP_ + j), in0=flat(core, Z_ + j), scalar=col("r_k", j), in1=flat(core, Z_ + 4 + j),
                        op0=ALU.mult, op1=ALU.mult), sem("bonus_in") if j == 3 else None)
        else:
            for b in range(2):
                sem("bonus_made").take(eng)
                did(tt(flat(core, BON_ + 2 * b, 2), bank[5 + b][:], flat(core, Z_ + 8 + 2 * b, 2), ALU.mult),
                    sem(f"dve_emptied{5 + b}"))

    def mask(c):
        kept = over(core.const("gmask", 2 * CH, CA), 4)
        for k, at in ((0, GM_), (1, GN_)):
            b = 3 + 2 * (c % 2) + k
            sem("chunk_made").take(eng)
            did(tt(flat(core, at + 2 * c, 2).rearrange("p (j n) -> p j n", j=4),
                   bank[b][:].rearrange("p (j n) -> p j n", j=4), kept, ALU.mult), sem(f"dve_emptied{b}"))
        if c == NCH - 1:
            line.tell(sem("masked"))

    def solve(s):
        if s == 0:
            eng.wait_ge(sem("inverses_in").sem, 256)
        else:
            for b in range(2):
                src = (5 if s % 2 else 3) + b
                sem("solved").take(eng) if s > 1 or b else sem("solved").take(eng, 3)
                did(tt(flat(core, NB_ + 2 * b, 2), bank[src][:], flat(core, UD_ + 2 * b, 2), ALU.add),
                    sem(f"dve_emptied{src}"))
            line.tell(core.sem("u_made"))

    def scan_y(c):
        if c == NCH - 1:
            return
        last = core.small[:, PC_:PC_ + 16].rearrange("p (j c) -> p j c", j=4)[:, :, c:c + 1].broadcast_to([P, 4, CH])
        state, following, ps, tmp = (x.rearrange("p (j v) -> p j v", j=4) for x in (
            flat(core, state_at(c)), flat(core, state_at(c + 1)), bank[5][:, 0:T], flat(core, STMP_)))
        sem("state_made").take(eng)
        if c:
            line.settled()
            did(tt(tmp, ps, state, ALU.add), sem("dve_emptied5"))
            line.settled()
            did(tt(following, tmp, last, ALU.mult), sem("state"))
        else:
            did(tt(following, ps, last, ALU.mult), sem("dve_emptied5"))
            line.tell(sem("state"))

    def gn(part):
        yc = flat(core, YC_, 4)
        if part == 0:
            for b in range(2):
                sem("y_mean").take(eng)
                did(stt(out=flat(core, YC_ + 2 * b, 2), in0=bank[3 + b][:], scalar=-1.0 / HD,
                        in1=flat(core, YT_ + 2 * b, 2), op0=ALU.mult, op1=ALU.add), sem(f"dve_emptied{3 + b}"))
            line.tell(core.sem("centred"))
            eng.wait_ge(sem("act_emptied5").sem, GN_USE_OF_5)
            did(eng.reciprocal(flat(core, SG_)[0:8, :], flat(core, TL_)[0:8, :]), sem("y_scale"))
        else:
            for b in range(2):
                sem("spread_made").take(eng)
                y2 = flat(core, YC_ + 2 * b, 2)
                did(tt(y2, bank[6 + b][:], y2, ALU.mult), sem(f"dve_emptied{6 + b}"))
            line.settled()
            for j in range(4):
                y1 = flat(core, YC_ + j)
                did(ts(y1, y1, col("ln_w", j), col("ln_b", j), ALU.mult, ALU.add))
            line.settled()
            did(tt(yc, yc, flat(core, BON_, 4), ALU.add))
            line.settled()
            did(tt(yc, yc, flat(core, G_, 4), ALU.mult), sem("yc"))
            low(0, 4, core.a(YC_, 4), "yc_high", "yc_ready")

    walk(SCHED_A, dict(params=lambda _: eng.wait_ge(sem("vec_in").sem, 16), split=split, norm=norm, unit=unit, conv=conv, rope=rope, w_idx=w_idx, isc=isc, topk=topk,
                       scores=scores, divide=divide, attn_out=attn_out, decay=decay, k_norm=k_norm, keys=keys, mask=mask,
                       solve=solve, scan_y=scan_y, gn=gn, ffn=ffn))


def state_at(c):
    return (S_, UD_)[c % 2]


def cu_tile(core):
    return core.ar[:, CU_ * T:CU_ * T + 4 * (T + 2)].rearrange("p (j t) -> p j t", j=4)


FFN_NORM_USE_OF_7 = 1 + 1 + 8 + 1 + 3 + 1
ISC_USES = [2 + k // 2 for k in range(8)]
LORA_USES_OF_3 = 1 + 4 + 1 + 1
GN_USE_OF_5 = 1 + 1 + 1


def rope_angles(core, line, positions, at):
    eng, did = line.eng, line.did
    ts, stt = eng.tensor_scalar, eng.scalar_tensor_tensor
    pos, n = flat(core, at + 4), flat(core, at + 5)
    parts, rest = [], TWO_PI
    for bits in (8, 12, 24):
        scale = 2.0 ** (bits - 1 - math.floor(math.log2(abs(rest))))
        parts.append(round(rest * scale) / scale)
        rest -= parts[-1]
    did(eng.tensor_copy(pos, positions))
    for r, name in ((0, "inv64"), (1, "inv32")):
        sin, cos = flat(core, 2 * r + 1), flat(core, 2 * r)
        line.settled()
        did(ts(sin, pos, core.const(name, 1, CA), None, ALU.mult))
        line.settled()
        did(ts(n, sin, 1.0 / TWO_PI, 12582912.0, ALU.mult, ALU.add))
        line.settled()
        did(ts(n, n, 12582912.0, None, ALU.subtract))
        for part in parts:
            line.settled()
            did(stt(out=sin, in0=n, scalar=-part, in1=sin, op0=ALU.mult, op1=ALU.add))
        line.settled()
        did(ts(cos, sin, math.pi / 2, None, ALU.add))
        line.settled()
        did(ts(n, cos, math.pi, -TWO_PI, ALU.is_gt, ALU.mult))
        line.settled()
        did(eng.tensor_tensor(cos, cos, n, ALU.add))
        line.settled()
        for x in (sin, cos):
            did(ts(x, x, 3.1415925, -3.1415925, ALU.min, ALU.max))
        line.settled()
        line.tell(core.sem("angles"))


def vector_program(core, eng):
    line, sem = Line(eng, core.sem("dve_steps")), core.sem
    for at, value in ((EPS_, RMS_EPS), (GNEPS_, GN_EPS), (SUBEPS_, SUBLN_EPS)):
        line.did(eng.memset(core.small[:, at:at + 1], value))
    for name in ("pos_in", "model_in"):
        eng.wait_ge(sem(name).sem, 16)
    rope_angles(core, line, flat(core, 6).bitcast(I32), 0)
    meet(core, line, PHASES["start"])
    core.fresh()
    with eng.Fori(0, core.layers_a) as layer:
        vector_a(core, eng, line)
        meet(core, line, layer + PHASES["a"])
    core.fresh()
    dve_norm(core, line, lambda k: core.const("final", 2 * KD)[:, k:k + 1], False, 1)(0)
    meet(core, line, PHASES["middle"])
    core.fresh()
    with eng.Fori(0, core.layers_b) as layer:
        vector_b(core, eng, line)
        meet(core, line, layer + PHASES["b"])
    core.fresh()
    dve_norm(core, line, lambda k: core.const("final", 2 * KD)[:, KD + k:KD + k + 1], False, 1)(0)


def gemm(eng, out, w, x, first, last):
    (wh, wl), (xh, xl) = w, x
    eng.matmul(out, wh, xh, start=first, stop=False, skip_group_check=True)
    eng.matmul(out, wh, xl, start=False, stop=False, skip_group_check=True)
    return eng.matmul(out, wl, xh, start=False, stop=last, skip_group_check=True)


class Banks:

    def __init__(self, core, eng):
        self.core, self.eng, self.held, self.count = core, eng, {}, {}

    def fill(self, b, reader):
        if b in self.held:
            r = self.held[b]
            self.eng.wait_ge(self.core.sem(f"{r}_emptied{b}").sem, self.count[b, r])
        self.held[b] = reader
        self.count[b, reader] = self.count.get((b, reader), 0) + 1
        return self.core.bank[b]


def pe_units(core, eng, rows, banks, inputs):
    sem = core.sem

    def unit(u):
        kind, i, _, _, fills = rows[u]
        eng.wait_ge(sem("slab_split").sem, u + 1)
        wh, wl = core.wh[u % PARTS][:], core.wl[u % PARTS][:]
        ntile = {"br": 4, "do": 8}.get(kind[:2], 2)
        nk = 16 // ntile
        wh, wl = (w.rearrange("p (k j m) -> p k j m", k=nk, j=ntile) for w in (wh, wl))

        def product(out, j, k, first, last):
            at = inputs[kind](i, k)
            return gemm(eng, out, (wh[:, k, j, :], wl[:, k, j, :]), (core.xh[:, at, :], core.xl[:, at, :]), first, last)

        if kind == "down":
            for j in range(8):
                bank = core.bank[3 + j // 2]
                if i == 0 and j % 2 == 0:
                    banks.fill(3 + j // 2, "dve")
                for k in range(2):
                    last = product(bank[:, (j % 2) * T:(j % 2) * T + T], j, k, i == 0 and k == 0 and j % 2 == 0,
                                   i == FT // 2 - 1 and k == 1)
            last.then_inc(sem("products").sem, 1)
            return
        for b, (bank, reader, _) in enumerate(fills):
            banks.fill(bank, reader)
            for j in range(1 if kind == "ki" else 2):
                for k in range(nk):
                    last = product(core.bank[bank][:, j * T:j * T + T], 2 * b + j, k, k == 0, k == nk - 1)
            last.then_inc(sem("products").sem, 1)

    return unit


def pe_square(core, eng, banks):
    def square(i):
        core.sem("squared").take(eng)
        if i == 0:
            banks.fill(7, "act")
        for k in range(2):
            ins = eng.matmul(core.bank[7][:, 0:T], core.const("ones"), flat(core, SQ_ + 2 * i + k), start=(i == 0 and k == 0),
                             stop=(i == 3 and k == 1))
        if i == 3:
            ins.then_inc(core.sem("mean_square").sem, 1)

    return square


def tensor_a(core, eng):
    rows, sem, banks, bank = PLAN_A, core.sem, Banks(core, eng), core.bank
    mm = eng.matmul

    def x_tile(i, k):
        if k % 2 == 0:
            sem("x_ready").at_least(eng, x_tile.base + k // 2 + 1)
        return k
    x_tile.base = 0

    def x_ffn(i, k):
        if i == 0 and k % 2 == 0:
            sem("x_ready").at_least(eng, 4 + k // 2 + 1)
        return k

    def y_tile(g, name, count, at):
        def tile(i, k):
            if i == 0 and k == 0:
                sem(name).at_least(eng, count)
            return at + k
        return tile

    def mixed(i, k):
        if k % 2 == 0:
            sem("mix_ready").at_least(eng, k // 2 + 1)
        return 4 + k

    def hidden(i, k):
        sem("hidden_low").at_least(eng, 2 * i + 2)
        return 8 + (2 * i + k) % 8

    inputs = {kind: x_tile for kind in ("q", "kv", "qi", "ki", "rz", "uc", "cb", "ga", "gb", "gc")}
    inputs |= {"br0": y_tile(0, "ya_done", 2, 8), "br1": y_tile(1, "yb_ready", 2, 12), "br2": y_tile(2, "yc_ready", 1, 0),
               "out": mixed, "up": x_ffn, "down": hidden}
    unit = pe_units(core, eng, rows, banks, inputs)

    def rope(r):
        at, n, b, table, source = ((0, 2, 3, "rot64", ("q", 0)), (2, 2, 4, "rot64", ("q", 1)), (4, 1, 5, "rot64", ("kv", 0)),
                                   (6, 2, 6, "rot32", ("qi", 0)), (8, 1, 7, "rot32", ("ki", 0)))[r]
        emptied(core, eng, rows, UA[source])
        banks.fill(b, "dve")
        mm(bank[b][:, 0:n * T], core.const(table, table=CC if table == "rot64" else CA), flat(core, QK_ + at, n),
           start=True, stop=True).then_inc(sem("swapped").sem, 1)

    def v_tok(_):
        emptied(core, eng, rows, UA["kv", 0])
        banks.fill(7, "act")
        for s in range(2):
            ins = eng.transpose(bank[7][:, s * P:s * P + P], flat(core, QK_ + 5)[:, s * P:s * P + P], core.const("ident"))
        ins.then_inc(sem("v_turned").sem, 1)

    def w_idx(_):
        emptied(core, eng, rows, UA["ki", 0])
        banks.fill(7, "dve")
        for s in range(2):
            ins = eng.transpose(bank[7][:, s * P:s * P + P], flat(core, QK_ + 8)[:, s * P:s * P + P], core.const("ident"))
        ins.then_inc(sem("w_turned").sem, 1)

    def k_pad(n):
        sem("rotated").at_least(eng, 3)
        banks.fill(3 + n, "act")
        for p in range(2):
            ins = mm(bank[3 + n][:, p * T:p * T + T], core.const("dup", 512, CA)[:, (2 * n + p) * P:][:, 0:P],
                     flat(core, QK_ + 4), start=True, stop=True)
        ins.then_inc(sem("k_padded").sem, 1)

    def ki_pad(_):
        sem("rotated").at_least(eng, 5)
        for n in range(2):
            banks.fill(5 + n, "act")
            for p in range(2):
                ins = mm(bank[5 + n][:, p * T:p * T + T], core.const("rep", 224, CA)[:, 96 - 32 * (2 * n + p):][:, 0:P],
                         flat(core, QK_ + 8), start=True, stop=True)
            ins.then_inc(sem("ki_padded").sem, 1)

    def isc(k):
        m, pair, width = k // 4, k % 4, WIDTH[k // 4]
        if k == 0:
            eng.wait_ge(sem("act_emptied6").sem, 1)
        b = 3 + k % 2
        banks.fill(b, "act")
        mm(heads(bank[b], width), flat(core, QK_ + 6 + pair // 2)[:, m * P:m * P + P],
           core.a(KI_ + 2 * (pair % 2), 2)[:, :, 0:width], start=True, stop=True).then_inc(sem("index_scores").sem, 1)

    def scores(k):
        m, pair, width = k // 4, k % 4, WIDTH[k // 4]
        banks.fill(5 + k % 2, "dve")
        mm(heads(bank[5 + k % 2], width), flat(core, QK_ + pair)[:, m * P:m * P + P],
           core.a(KZ_ + 2 * (pair // 2), 2)[:, :, 0:width], start=True, stop=True).then_inc(sem("scored").sem, 1)

    def turn(k):
        m, width = k // 4, WIDTH[k // 4]
        sem("exps").take(eng)
        banks.fill(7, "act")
        buf = heads(flat(core, SC_ + 2 * (k % 2), 2), width)
        for p in range(2):
            for s in range(m + 1):
                n = p * (m + 1) + s
                ins = eng.transpose(bank[7][:, n * P:n * P + P], buf[:, p, s * P:s * P + P], core.const("ident"))
        ins.then_inc(sem("turned").sem, 1)
        turn.at[k] = banks.count[7, "act"]
    turn.at = {}

    def pv(k):
        m, pair = k // 4, k % 4
        eng.wait_ge(sem("act_emptied7").sem, turn.at[k])
        if pair == 0:
            banks.fill(3 + m, "dve")
        for p in range(2):
            h = 2 * pair + p
            for s in range(m + 1):
                n = p * (m + 1) + s
                ins = mm(bank[3 + m][:, h * HD:h * HD + HD], flat(core, PT_ + 2 * (k % 2), 2)[:, n * P:n * P + P],
                         flat(core, VT_)[:, s * P + HD * (pair // 2):][:, 0:HD], start=(s == 0), stop=(s == m),
                         skip_group_check=True)
        ins.then_inc(sem("weighted").sem, 1)

    def attn_out(m):
        sem("divided").take(eng)
        banks.fill(7, "dve")
        for j in range(4):
            ins = eng.transpose(bank[7][:, j * P:j * P + P], flat(core, OS_, 2)[:, j * P:j * P + P], core.const("ident"))
        ins.then_inc(sem("outputs_turned").sem, 1)

    def lora(_):
        sem("lora_inputs").take(eng)
        eng.wait_ge(sem("lora_in").sem, 16)
        for half in range(2):
            rows_, x = slice(64 * half, 64 * half + 64), flat(core, (TL_, Z_ + 12)[half])
            for b in range(2):
                banks.fill(3 + 2 * half + b, "act")
                for k in range(2):
                    j = 2 * b + k
                    ins = mm(bank[3 + 2 * half + b][:, k * T:k * T + T], core.lora[rows_, j * P:j * P + P], x[rows_, :],
                             start=True, stop=True)
                ins.then_inc(sem("lora_made").sem, 1)
        for b, dst in ((0, 7), (1, 3)):
            banks.fill(dst, "act")
            for k in range(2):
                j = 2 * b + k
                ins = mm(bank[dst][:, k * T:k * T + T], core.lora[:, 512 + j * P:][:, 0:P], flat(core, SG_), start=True,
                         stop=True)
            ins.then_inc(sem("lora_made").sem, 1)

    def head_sums(src, b, reader, tally):
        banks.fill(b, reader)
        for j in range(4):
            ins = mm(bank[b][0:8, 0:T], core.const("sel", 32, CA)[:, 8 * j:8 * j + 8], flat(core, src + j), start=(j == 0),
                     stop=(j == 3))
        ins.then_inc(sem(tally).sem, 1)

    def spread(src):
        for b in range(2):
            banks.fill(6 + b, "dve")
            for k in range(2):
                j = 2 * b + k
                ins = mm(bank[6 + b][:, k * T:k * T + T], core.const("spread", 512, CA)[0:8, j * P:j * P + P],
                         flat(core, src)[0:8, :], start=True, stop=True)
            ins.then_inc(sem("spread_made").sem, 1)

    def k_norm(part):
        if part == 0:
            sem("kk_squared").take(eng)
            head_sums(TMP_, 5, "dve", "kk_summed")
        else:
            sem("k_scale").take(eng)
            spread(TL_)

    def keys(part):
        if part == 1:
            sem("bonus_in").take(eng)
            for b in range(2):
                banks.fill(5 + b, "dve")
                mm(bank[5 + b][:], core.const("blk"), flat(core, TMP_ + 2 * b, 2), start=True, stop=True).then_inc(
                    sem("bonus_made").sem, 1)

    def half(ap, p):
        return ap[HD * p:HD * p + HD]

    def chunk(c):
        if c == 0:
            sem("keys_ready").take(eng)
        ar = core.a(PV_, 8).rearrange("p (a j) t -> p a j t", a=2)
        for k, src in ((0, KK_), (1, PI_)):
            b = 3 + 2 * (c % 2) + k
            banks.fill(b, "dve")
            out = bank[b][:].rearrange("p (j a t) -> p j a t", j=4, a=2)
            for j in range(4):
                for p in range(2):
                    ins = mm(half(out[:, j], p), half(flat(core, src + j), p)[:, c * CH:c * CH + CH],
                             half(ar[:, :, j, c * CH:c * CH + CH], p), start=True, stop=True, skip_group_check=True)
            ins.then_inc(sem("chunk_made").sem, 1)

    def tok(x):
        src = (Z_ + 8, KK_, PI_)[x]
        for b in range(2):
            banks.fill((7, 3)[b], "act")
            out = bank[(7, 3)[b]][:].rearrange("p (c j v) -> p c j v", c=2, j=4)
            for c2 in range(2):
                for j in range(4):
                    for p in range(2):
                        at = (2 * b + c2) * CH
                        ins = mm(half(out[:, c2, j, :], p), half(flat(core, src + j), p)[:, at:at + CH],
                                 half(core.const("ident"), p)[:, HD * p:HD * p + HD], start=True, stop=True,
                                 skip_group_check=True)
            ins.then_inc(sem("tok_made").sem, 1)

    def of(at, cj, p):
        return half(flat(core, at, 4)[:, cj * CH:cj * CH + CH], p)

    def q2t(cj, p):
        return half(flat(core, (Q2A_, Q2B_)[cj // 8], 2)[:, (cj % 8) * CH:(cj % 8) * CH + CH], p)

    def solve(s):
        if s == 0:
            eng.wait_ge(sem("inverses_in").sem, 256)
            sem("off_diagonal").take(eng)
        elif s == 1:
            for b in range(2):
                eng.wait_ge(sem(f"act_emptied{3 + b}").sem, banks.count[3 + b, "act"])
        else:
            sem("u_made").take(eng)
        for b in range(2):
            dst = (5 if s % 2 else 3) + b
            banks.fill(dst, "dve" if s else "act")
            for cj in range(8 * b, 8 * b + 8):
                for p in range(2):
                    out = half(bank[dst][:, (cj % 8) * CH:(cj % 8) * CH + CH], p)
                    if s == 0:
                        ins = mm(out, of(NB_, cj, p), of(TD_, cj, p), start=True, stop=True, skip_group_check=True)
                    else:
                        ins = mm(out, q2t(cj, p), of(UD_ if s == 1 else NB_, cj, p), start=True, stop=True,
                                 skip_group_check=True)
            ins.then_inc(sem("solved").sem, 1)

    def gram(at, cj, a, p):
        return half(flat(core, at, 8)[:, cj * 2 * CH + a * CH:][:, 0:CH], p)

    def small(at, j, p):
        return half(flat(core, at)[:, j * HD:j * HD + HD], p)

    def scan_rhs(c):
        if c == 0:
            sem("u_made").take(eng)
        banks.fill(3, "act")
        for j in range(4):
            for p in range(2):
                ins = mm(half(bank[3][:, j * HD:j * HD + HD], p), gram(GN_, 4 * c + j, 0, p), of(VTOK_, 4 * c + j, p),
                         start=(j == 0), stop=(c == 0), skip_group_check=True)
        if c:
            sem("state").take(eng)
            for j in range(4):
                for p in range(2):
                    ins = mm(half(bank[3][:, j * HD:j * HD + HD], p), half(flat(core, PV_ + j), p)[:, c * CH:c * CH + CH],
                             small(state_at(c), j, p), start=False, stop=True, skip_group_check=True)
        ins.then_inc(sem("rhs_made").sem, 1)

    def scan_sa(c):
        eng.wait_ge(sem("act_emptied3").sem, banks.count[3, "act"])
        banks.fill(4, "act")
        for j in range(4):
            for p in range(2):
                ins = mm(half(bank[4][:, j * HD:j * HD + HD], p), of(NB_, 4 * c + j, p), small(RHS_, j, p), start=True,
                         stop=True, skip_group_check=True)
        ins.then_inc(sem("sa_made").sem, 1)

    def scan_y(c):
        eng.wait_ge(sem("act_emptied4").sem, banks.count[4, "act"])
        if c < NCH - 1:
            banks.fill(5, "dve")
            for j in range(4):
                for p in range(2):
                    out, cj = half(bank[5][:, j * HD:j * HD + HD], p), 4 * c + j
                    mm(out, of(Z_, cj, p), small(SA_, j, p), start=True, stop=False, skip_group_check=True)
                    ins = mm(out, of(Z_ + 4, cj, p), of(VTOK_, cj, p), start=False, stop=True, skip_group_check=True)
            ins.then_inc(sem("state_made").sem, 1)
        banks.fill(6, "act")
        for j in range(4):
            for p in range(2):
                out, cj = half(bank[6][:, j * CH:j * CH + CH], p), 4 * c + j
                if c:
                    mm(out, small(state_at(c), j, p), half(flat(core, A_ + j), p)[:, c * CH:c * CH + CH], start=True,
                       stop=False, skip_group_check=True)
                mm(out, small(SA_, j, p), gram(GM_, cj, 1, p), start=(c == 0), stop=False, skip_group_check=True)
                ins = mm(out, of(VTOK_, cj, p), gram(GN_, cj, 1, p), start=False, stop=True, skip_group_check=True)
        ins.then_inc(sem("y_made").sem, 1)

    def gn(part):
        if part == 0:
            eng.wait_ge(sem("act_emptied6").sem, banks.count[6, "act"])
            for b in range(2):
                banks.fill(3 + b, "dve")
                mm(bank[3 + b][:], core.const("blk"), flat(core, YT_ + 2 * b, 2), start=True, stop=True).then_inc(
                    sem("y_mean").sem, 1)
            sem("y_squared").take(eng)
            head_sums(YSQ_, 5, "act", "y_variance")
        else:
            sem("y_scale").take(eng)
            spread(SG_)

    walk(SCHED_A, dict(unit=unit, square=pe_square(core, eng, banks), rope=rope, v_tok=v_tok, w_idx=w_idx, k_pad=k_pad,
                       ki_pad=ki_pad, isc=isc, scores=scores, turn=turn, pv=pv, attn_out=attn_out, lora=lora,
                       k_norm=k_norm, keys=keys, chunk=chunk, tok=tok, solve=solve, scan_rhs=scan_rhs, scan_sa=scan_sa,
                       scan_y=scan_y, gn=gn))


def tensor_program(core, eng):
    line = Line(eng, core.sem("pe_steps"))

    eng.wait_ge(core.sem("const_in").sem, 16)
    meet(core, line, PHASES["start"])
    core.fresh()
    with eng.Fori(0, core.layers_a) as layer:
        tensor_a(core, eng)
        line.last = (core.sem("products").sem, PLAN_A[-1][3])
        meet(core, line, layer + PHASES["a"])
    core.fresh()
    square = pe_square(core, eng, Banks(core, eng))
    for i in range(4):
        square(i)
    eng.wait_ge(core.sem("mean_square").sem, 1)
    meet(core, line, PHASES["middle"])
    core.fresh()
    with eng.Fori(0, core.layers_b) as layer:
        tensor_b(core, eng)
        line.last = (core.sem("products").sem, PLAN_B[-1][3])
        meet(core, line, layer + PHASES["b"])
    core.fresh()
    square = pe_square(core, eng, Banks(core, eng))
    for i in range(4):
        square(i)
    eng.wait_ge(core.sem("mean_square").sem, 1)


def pool_a(core, eng, line):
    sem, did = core.sem, line.did

    def invert(_):
        ut = flat(core, UT_, 2).rearrange("p (w i t) -> p w i t", w=2, i=SUB)
        n = flat(core, BD_).rearrange("p (i t) -> p i t", i=SUB)
        u, prod = ut[:, 0], flat(core, PROD_)
        sem("masked").at_least(eng, 1)
        did(eng.memset(flat(core, UT_, 2), 0.0))
        line.settled()
        did(eng.memset(flat(core, UT_)[:, 0:T:SUB + 1], 1.0))
        eng.wait_ge(sem("blocks_in").sem, 16)
        for j in range(SUB - 1, 0, -1):
            m = SUB - j
            term = prod[:, 0:j * m].rearrange("p (i t) -> p i t", i=j)
            above = u[:, 0:j, j:SUB]
            line.settled()
            did(eng.tensor_tensor(term, n[:, 0:j, j:j + 1].broadcast_to([P, j, m]),
                                  u[:, j:j + 1, j:SUB].broadcast_to([P, j, m]), ALU.mult))
            line.settled()
            did(eng.tensor_tensor(above, above, term, ALU.add))
        line.settled()
        did(eng.tensor_copy(ut[:, 1], u.rearrange("p i t -> p t i")))
        line.tell(sem("inverted"))

    def off_diag(_):
        sem("tok_made").take(eng, 6)
        sem("masked").at_least(eng, 1)
        did(eng.memset(flat(core, UD_, 4), 0.0))
        did(eng.memset(flat(core, TD_, 4), 0.0))
        did(eng.tensor_tensor(flat(core, NB_, 4).rearrange("p (n t) -> p n t", n=16),
                              flat(core, GM_, 8).rearrange("p (n a t) -> p n a t", n=16, a=2)[:, :, 0, :],
                              over(core.const("off", CH, CA), 16), ALU.mult), sem("off_diagonal"))

    walk(SCHED_A, dict(invert=invert, off_diag=off_diag))


def pool_program(core, eng):
    line = Line(eng, core.sem("pool_steps"))
    meet(core, line, PHASES["start"], True)
    core.fresh()
    with eng.Fori(0, core.layers_a) as layer:
        pool_a(core, eng, line)
        meet(core, line, layer + PHASES["a"], True)
    core.fresh()
    meet(core, line, PHASES["middle"], True)
    core.fresh()
    with eng.Fori(0, core.layers_b) as layer:
        pool_b(core, eng, line)
        meet(core, line, layer + PHASES["b"], True)
    core.fresh()


PLANNED_B = {unit: PLAN_B[u] for u, unit in enumerate(UNITS_B)}


def scores_of(core, k):
    buf = flat(core, BSC_ + 3 * (k % 2), 3)
    return heads(buf, P), heads(buf[:, T:3 * T], T)


def turned_of(core, k):
    buf = flat(core, BPT_[k % 2], 3)
    return buf[:, 0:T], buf[:, T:3 * T]


def scalar_b(core, eng, line, earlier):
    rows, sem, bank, vec = PLAN_B, core.sem, core.bank, core.vec
    square, norm = act_norm(core, line, True)

    def act(out, in_, func, tally=None, **kw):
        line.did(eng.activation(out, in_, func, **kw), tally)

    def lam(_):
        sem("lam_sums").take(eng)
        act(core.small[:, 12:14], bank[6][:, 0:2], ACT.Exp, sem("act_emptied6"))

    def unit(u):
        kind, i, _, _, banks = rows[u]
        b = banks[0][0]
        second = kind.isupper()
        if kind in ("v", "V"):
            n = 4 * second + i
            made(core, eng, rows, u)
            if n >= 2:
                sem("v_turned").at_least(eng, n - 1)
            act(flat(core, BRAW_ + 2 * (i % 2), 2), bank[b][:], ACT.Copy, sem(f"act_emptied{b}"))
        elif kind in ("qk", "QK"):
            k = 8 * second + i
            made(core, eng, rows, u)
            if k >= 2:
                sem("scored").at_least(eng, k - 1)
            act(flat(core, BX_ + 2 * (i % 2), 2), bank[b][:], ACT.Copy, sem(f"act_emptied{b}"))
        elif kind in ("z", "Z", "g", "G"):
            made(core, eng, rows, u)
            at = (BZ_ if kind in "zZ" else BG_)[second]
            act(flat(core, at + 2 * i, 2), bank[b][:], ACT.Copy, sem(f"act_emptied{b}"))
        elif kind == "pb":
            sem("merged").take(eng)
            act(core.xh[:, 8 + 2 * i:10 + 2 * i, :], core.a(BG_[0] + 2 * i, 2), ACT.Copy, sem("merged_high"))

    def v_turn(n):
        sem("v_turned").take(eng)
        act(flat(core, BV_[n // 4] + 2 * (n % 4), 2), bank[5][:], ACT.Copy, sem("act_emptied5"))

    def scores(k):
        sem("maxed").take(eng)
        for m, buf in enumerate(scores_of(core, k)):
            for p in range(2):
                c = 2 * m + p
                act(buf[:, p, :], buf[:, p, :], ACT.Exp, sem("exps") if c == 3 else None,
                    bias=core.small[:, 136 + 4 * (k % 2) + c:][:, 0:1],
                    accum_out=core.small[:, DEN_ + 4 * (k % 4) + c:][:, 0:1])

    def turn(k):
        for m, (b, n) in enumerate(((6, T), (5, 2 * T))):
            sem("turned").take(eng)
            if k >= 2 and m == 0:
                sem("weighted").at_least(eng, k - 1)
            act(turned_of(core, k)[m], bank[b][:, 0:n], ACT.Copy, sem(f"act_emptied{b}"))

    def silu(kind):
        line.settled()
        z = flat(core, BZ_[kind], 8)
        act(z, z, ACT.Silu, sem("z_ready"))

    def rms(_):
        sem("outputs_done").take(eng)
        act(flat(core, BSQ_, 8), flat(core, BO_, 8), ACT.Square, sem("outputs_squared"))
        sem("outputs_summed").take(eng)
        act(core.small[:, 160:176], core.small[:, 144:160], ACT.Sqrt, sem("outputs_rooted"),
            bias=core.small[:, SUBEPS_:SUBEPS_ + 1], scale=1.0 / (2 * HD))

    def post(n):
        kind, i = n // 4, n % 4
        sem("y_made").take(eng)
        at = 8 * (1 - kind) + 2 * i
        act(core.xh[:, at:at + 2, :], core.a(BY_[kind] + 2 * (i % 2), 2), ACT.Copy, sem("y_high"))

    def gate(g):
        line.settled()
        x = flat(core, BG_[g], 8)
        act(x, x, ACT.Sigmoid, sem("gated"))

    walk(SCHED_B, dict(round=act_round(core, line, rows, earlier), square=square, norm=norm, lam=lam, unit=unit, v_turn=v_turn,
                       scores=scores, turn=turn, silu=silu, rms=rms, post=post, gate=gate))


def vector_b(core, eng, line):
    rows, sem, bank, vec, did = PLAN_B, core.sem, core.bank, core.vec, line.did
    tt, ts, stt = eng.tensor_tensor, eng.tensor_scalar, eng.scalar_tensor_tensor
    gain = lambda k: vec[:, VB["norm"] + k:][:, 0:1]

    def lam(_):
        q = vec[:, VB["lam"]:][:, 0:4].rearrange("p (n two) -> p n two", two=2)
        did(tt(core.small[:, 14:16].unsqueeze(2), q[:, :, 0:1], q[:, :, 1:2], ALU.mult), sem("lam_products"))
        eng.wait_ge(sem("act_emptied6").sem, 1)
        did(tt(core.small[:, LAM_:LAM_ + 1], core.small[:, 13:14], core.small[:, 12:13], ALU.subtract))
        line.settled()
        did(tt(core.small[:, LAM_:LAM_ + 1], core.small[:, LAM_:LAM_ + 1], vec[:, VB["lam_init"]:][:, 0:1], ALU.subtract))
        did(ts(core.small[:, LAM_ + 1:LAM_ + 2], vec[:, VB["subln"]:][:, 0:1], vec[:, VB["lam_init"] + 1:][:, 0:1], None,
               ALU.mult))

    def unit(u):
        kind, i, _, _, banks = rows[u]
        if kind in ("pa", "pb"):
            if i == 0:
                sem("gated").take(eng)
            b = banks[0][0]
            g = flat(core, BG_[kind == "pb"] + 2 * i, 2)
            made(core, eng, rows, u)
            did(tt(g, bank[b][:], g, ALU.mult), sem(f"dve_emptied{b}"))
            if kind == "pb":
                line.settled()
                total = flat(core, BG_[0] + 2 * i, 2)
                did(tt(total, total, g, ALU.add), sem("merged"))
                sem("merged_high").take(eng)
                did(tt(core.xl[:, 8 + 2 * i:10 + 2 * i, :], core.a(BG_[0] + 2 * i, 2),
                       core.xh[:, 8 + 2 * i:10 + 2 * i, :].bitcast(F32), ALU.subtract), sem("merged_low"))
        elif kind == "out":
            made(core, eng, rows, u)
            res = core.h[:, 2 * i:2 * i + 2, :]
            did(tt(res, heads(bank[banks[0][0]], T), res, ALU.add), sem(f"dve_emptied{banks[0][0]}"))

    def swap(k):
        i = k % 8
        x, tmp, kz = core.a(BX_ + 2 * (k % 2), 2), core.a(BTMP_, 2), core.a(BKZ_ + 2 * (k % 2), 2)
        sem("swapped").take(eng)
        line.settled()
        did(tt(tmp, heads(bank[7], T), over(core.const("sin", T, CB), 2), ALU.mult), sem("dve_emptied7"))
        did(tt(x, x, over(core.const("cos", T, CB), 2), ALU.mult))
        line.settled()
        did(tt(x[:, 0], x[:, 0], tmp[:, 0], ALU.add))
        if k >= 2:
            sem("scored").at_least(eng, k - 1)
        for p in range(2):
            r = slice(HD * p, HD * p + HD)
            did(tt(kz[r, p], x[r, 1], tmp[r, 1], ALU.add), sem("rotated") if p else None)

    def scores(k):
        sem("scored").take(eng)
        if k >= 2:
            sem("turned").at_least(eng, 2 * k - 2)
        masks = [core.const("dilated", 384, CB)[:, m * P:][:, 0:WIDTH[m]] if k < 8 else core.causal(m) for m in range(2)]
        mx = core.small[:, 136 + 4 * (k % 2):][:, 0:4]
        line.settled()
        for m, buf in enumerate(scores_of(core, k)):
            width = WIDTH[m]
            did(stt(out=buf, in0=heads(bank[3 + m], width), scalar=HD ** -0.5, in1=over(masks[m], 2),
                    op0=ALU.mult, op1=ALU.add), sem(f"dve_emptied{3 + m}"))
        line.settled()
        for m, buf in enumerate(scores_of(core, k)):
            did(eng.tensor_reduce(mx[:, 2 * m:2 * m + 2], buf, AX_X, ALU.max))
        line.settled()
        did(ts(mx, mx, -1.0, None, ALU.mult), sem("maxed"))

    def pv(k):
        kind, i = k // 8, k % 8
        sem("weighted").take(eng)
        rden = core.small[:, RDEN_:RDEN_ + 4]
        line.settled()
        did(eng.reciprocal(rden, core.small[:, DEN_ + 4 * (k % 4):][:, 0:4]))
        line.settled()
        if kind == 0:
            did(tt(flat(core, BO_ + i).rearrange("p (n d) -> p n d", n=4), bank[7][:, 0:T].rearrange("p (n d) -> p n d", n=4),
                   rden.unsqueeze(2).broadcast_to([P, 4, HD]), ALU.mult), sem("dve_emptied7"))
            return
        r2 = rden.rearrange("p (m n) -> p m n", m=2)
        did(ts(r2[:, :, 1:2], r2[:, :, 1:2], core.small[:, LAM_:LAM_ + 1], None, ALU.mult))
        line.settled()
        o = bank[7][:].rearrange("p (m n d) -> p m n d", m=2, n=2)
        two = [flat(core, BTMP_ + n).rearrange("p (m d) -> p m d", m=2) for n in range(2)]
        for n in range(2):
            did(tt(two[n], o[:, :, n, :], r2[:, :, n:n + 1].broadcast_to([P, 2, P]), ALU.mult),
                sem("dve_emptied7") if n else None)
        line.settled()
        if k == 8:
            sem("outputs_turned").at_least(eng, 4)
        did(tt(flat(core, BO_ + i).rearrange("p (m d) -> p m d", m=2), two[0], two[1], ALU.add),
            sem("outputs_done") if k == 15 else None)

    def rms(_):
        sem("outputs_squared").take(eng)
        did(eng.tensor_reduce(core.small[:, 144:160], flat(core, BSQ_, 8).rearrange("p (n d) -> p n d", n=16), AX_X,
                              ALU.add), sem("outputs_summed"))
        sem("outputs_rooted").take(eng)
        did(eng.reciprocal(core.small[:, 176:192], core.small[:, 160:176]))
        line.settled()
        o = flat(core, BO_, 8).rearrange("p (n d) -> p n d", n=16)
        did(tt(o, o, core.small[:, 176:192].unsqueeze(2).broadcast_to([P, 16, P]), ALU.mult), sem("outputs_scaled"))

    def post(n):
        kind, i = n // 4, n % 4
        y, z = flat(core, BY_[kind] + 2 * (i % 2), 2), flat(core, BZ_[kind] + 2 * i, 2)
        if i == 0:
            sem("z_ready").take(eng)
        sem("outputs_turned").take(eng)
        line.settled()
        if kind:
            did(stt(out=y, in0=bank[6 + i % 2][:], scalar=core.small[:, LAM_ + 1:LAM_ + 2], in1=z, op0=ALU.mult, op1=ALU.mult),
                sem(f"dve_emptied{6 + i % 2}"))
        else:
            did(tt(y, bank[6 + i % 2][:], z, ALU.mult), sem(f"dve_emptied{6 + i % 2}"))
        line.tell(sem("y_made"))
        sem("y_high").take(eng)
        at = 8 * (1 - kind) + 2 * i
        did(tt(core.xl[:, at:at + 2, :], core.a(BY_[kind] + 2 * (i % 2), 2), core.xh[:, at:at + 2, :].bitcast(F32),
               ALU.subtract), sem("y_low"))

    did(eng.memset(flat(core, BKZ_, 4), 0.0))
    walk(SCHED_B, dict(params=lambda _: eng.wait_ge(sem("vec_in").sem, 16), split=dve_split(core, line), norm=dve_norm(core, line, gain, True, 1), lam=lam, unit=unit, swap=swap,
                       scores=scores, pv=pv, rms=rms, post=post))


def tensor_b(core, eng):
    rows, sem, banks, bank = PLAN_B, core.sem, Banks(core, eng), core.bank
    mm = eng.matmul

    def x_tile(i, k):
        if k % 2 == 0:
            sem("x_ready").at_least(eng, k // 2 + 1)
        return k

    def y_tile(kind, base):
        def tile(i, k):
            if i == 0 and k % 2 == 0:
                sem("y_low").at_least(eng, 4 * kind + k // 2 + 1)
            return base + k
        return tile

    def merged(i, k):
        if k % 2 == 0:
            sem("merged_low").at_least(eng, k // 2 + 1)
        return 8 + k

    inputs = {kind: x_tile for kind in ("v", "V", "qk", "QK", "z", "Z", "g", "G")}
    inputs |= {"pa": y_tile(0, 8), "pb": y_tile(1, 0), "out": merged}

    def lam(_):
        sem("lam_products").take(eng)
        banks.fill(6, "act")
        mm(bank[6][:, 0:2], core.const("ones"), core.small[:, 14:16], start=True, stop=True).then_inc(sem("lam_sums").sem, 1)

    def v_turn(n):
        emptied(core, eng, rows, UB["Vv"[n < 4], n % 4])
        banks.fill(5, "act")
        for j in range(2):
            for s in range(2):
                ins = eng.transpose(bank[5][:, j * T + s * P:][:, 0:P], flat(core, BRAW_ + 2 * (n % 2) + j)[:, s * P:s * P + P],
                                    core.const("ident"))
        ins.then_inc(sem("v_turned").sem, 1)

    def swap(k):
        emptied(core, eng, rows, UB[("qk", "QK")[k // 8], k % 8])
        banks.fill(7, "dve")
        mm(bank[7][:], core.const("rot64"), flat(core, BX_ + 2 * (k % 2), 2), start=True, stop=True).then_inc(
            sem("swapped").sem, 1)

    def scores(k):
        sem("rotated").take(eng)
        for m in range(2):
            width = WIDTH[m]
            banks.fill(3 + m, "dve")
            ins = mm(heads(bank[3 + m], width), flat(core, BX_ + 2 * (k % 2))[:, m * P:m * P + P],
                     core.a(BKZ_ + 2 * (k % 2), 2)[:, :, 0:width], start=True, stop=True)
        ins.then_inc(sem("scored").sem, 1)

    def turn(k):
        sem("exps").take(eng)
        for m, b in enumerate((6, 5)):
            buf = scores_of(core, k)[m]
            banks.fill(b, "act")
            for p in range(2):
                for s in range(m + 1):
                    n = p * (m + 1) + s
                    ins = eng.transpose(bank[b][:, n * P:n * P + P], buf[:, p, s * P:s * P + P], core.const("ident"))
            ins.then_inc(sem("turned").sem, 1)
            turn.at[k] = banks.count[b, "act"]
    turn.at = {}

    def pv(k):
        kind, i = k // 8, k % 8
        eng.wait_ge(sem("act_emptied5").sem, turn.at[k])
        banks.fill(7, "dve")
        v, dim = flat(core, BV_[kind] + i), HD * (kind + 1)
        for m in range(2):
            for p in range(2):
                out = bank[7][:, (2 * m + p) * dim:][:, 0:dim]
                for s in range(m + 1):
                    n = p * (m + 1) + s
                    ins = mm(out, turned_of(core, k)[m][:, n * P:n * P + P],
                             v[:, s * P + (0 if kind else HD * p):][:, 0:dim], start=(s == 0), stop=(s == m),
                             skip_group_check=True)
        ins.then_inc(sem("weighted").sem, 1)

    def post(n):
        kind, i = n // 4, n % 4
        if n == 0:
            eng.wait_ge(sem("dve_emptied7").sem, 16)
        if n == 4:
            sem("outputs_scaled").take(eng)
        b = 6 + i % 2
        banks.fill(b, "dve")
        for j in range(2):
            for m in range(2):
                ins = eng.transpose(bank[b][:, j * T + m * P:][:, 0:P], flat(core, BO_ + 2 * i + j)[:, m * P:m * P + P],
                                    core.const("ident"))
        ins.then_inc(sem("outputs_turned").sem, 1)

    walk(SCHED_B, dict(square=pe_square(core, eng, banks), lam=lam, unit=pe_units(core, eng, rows, banks, inputs),
                       v_turn=v_turn, swap=swap, scores=scores, turn=turn, pv=pv, post=post))


def pool_b(core, eng, line):
    pass


def build(nc, dram, out, layers_a=LAYERS, layers_b=LAYERS):
    with ExitStack() as ctx:
        core = Core(nc, ctx, dram, out)
        core.layers_a, core.layers_b = layers_a, layers_b
        block = ctx.enter_context(nc.Block())

        @block.sync
        def _(eng):
            sync_program(core, eng)

        @block.scalar
        def _(eng):
            core.fresh()
            scalar_program(core, eng)

        @block.vector
        def _(eng):
            core.fresh()
            vector_program(core, eng)

        @block.tensor
        def _(eng):
            core.fresh()
            tensor_program(core, eng)

        @block.gpsimd
        def _(eng):
            core.fresh()
            pool_program(core, eng)


def constant_table():
    ident = np.eye(P, dtype=np.float32)
    r = np.arange(P)

    def rotation(dim):
        half, at = dim // 8, r % dim
        m = np.zeros((P, P), np.float32)
        lo, hi = r[at < half], r[(at >= half) & (at < 2 * half)]
        m[lo + half, lo] = -1.0
        m[hi - half, hi] = 1.0
        return m

    def dilated(m):
        dist = (m * P + r)[:, None] - np.arange(P * (m + 1))[None, :]
        count = sum(((dist % d == 0) & (dist <= w)).astype(np.int32) for w, d in ((128, 1), (512, 4), (2048, 16)))
        count = np.where(dist >= 0, count, 0)
        return np.where(count > 0, np.log(np.maximum(count, 1)), NEG).astype(np.float32)

    common = np.zeros((P, NCC), np.float32)
    common[:, CC["ident"]:][:, :P] = ident
    common[:, CC["ones"]:][:, :P] = 1.0
    common[:, CC["blk"]:][:, :P] = r[:, None] // HD == r[None, :] // HD
    common[:, CC["rot64"]:][:, :P] = rotation(HD)
    common[:, CC["causal"] + P:][:, :P] = np.where(r[None, :] <= r[:, None], 0.0, NEG)
    a = np.zeros((P, NCA), np.float32)
    a[:, CA["rot32"]:][:, :P] = rotation(IDX_DIM)
    a[np.arange(32), CA["rep"] + 96 + np.arange(32)] = 1.0
    for n in range(2):
        for p in range(2):
            a[64 * n + np.arange(64), CA["dup"] + P * (2 * n + p) + 64 * p + np.arange(64)] = 1.0
    inv64 = np.float32(500000.0) ** (-np.arange(8, dtype=np.float32) * np.float32(2.0) / np.float32(16))
    inv32 = np.float32(500000.0) ** (-np.arange(4, dtype=np.float32) * np.float32(2.0) / np.float32(8))
    a[:, CA["inv64"]] = np.where(r % 64 < 16, inv64[r % 8], 0.0)
    a[:, CA["inv32"]] = np.where(r % 32 < 8, inv32[r % 4], 0.0)
    s, t = r[:, None] % CH, np.arange(CH)[None, :]
    a[:, CA["gmask"]:][:, :CH] = s < t
    a[:, CA["gmask"] + CH:][:, :CH] = s <= t
    a[:, CA["off"]:][:, :CH] = s // SUB != t // SUB
    for j in range(4):
        a[r, CA["sel"] + 8 * j + 2 * j + r // HD] = 1.0
        for p in range(2):
            a[2 * j + p, CA["spread"] + P * j + 64 * p:][:64] = 1.0
    b = np.zeros((P, NCB), np.float32)
    b[:, CB["dilated"]:][:, :384] = np.concatenate([dilated(0), dilated(1)], 1)
    inv = np.float32(1.0) / (np.float32(500000.0) ** (np.arange(0, 16, 2, dtype=np.float32) / np.float32(16)))
    ang = np.where(r % 64 < 16, inv[r % 8], np.float32(0.0))[:, None] * np.arange(T, dtype=np.float32)[None, :]
    b[:, CB["cos"]:][:, :T] = np.cos(ang)
    b[:, CB["sin"]:][:, :T] = np.sin(ang)
    return common, a, b


def tiles(w, starts):
    w = w.reshape(w.shape[0] // P, P, w.shape[1])
    out = np.zeros((P, w.shape[0], len(starts), P), w.dtype)
    for j, s in enumerate(starts):
        if s is not None:
            out[:, :, j, :] = w[:, :, s:s + P].transpose(1, 0, 2)
    return out.reshape(P, -1)


def stream_a(w_in, w_branch, w_out, ffn_up, ffn_down):
    start = {"q": Q0, "kv": K0, "qi": QI0, "rz": RW0, "cb": B0, "ga": GATE0, "gb": GATE0 + D, "gc": GATE0 + 2 * D}
    slabs = np.zeros((LAYERS, len(UNITS_A), P, 2048), np.float32)
    for layer in range(LAYERS):
        for u, (kind, i) in enumerate(UNITS_A):
            if kind in start:
                s = tiles(w_in[layer], [start[kind] + 256 * i, start[kind] + 256 * i + P])
            elif kind == "ki":
                s = tiles(w_in[layer], [KI0, None])
            elif kind == "uc":
                s = tiles(w_in[layer], [U0 + P * i, C0 + P * i])
            elif kind.startswith("br"):
                s = tiles(w_branch[layer, int(kind[2])], [512 * i + P * j for j in range(4)])
            elif kind == "out":
                s = tiles(w_out[layer], [256 * i, 256 * i + P])
            elif kind == "up":
                s = tiles(ffn_up[layer], [P * i, D_FF + P * i])
            else:
                s = tiles(ffn_down[layer, 256 * i:256 * i + 256], [P * j for j in range(8)])
            slabs[layer, u] = s
    return slabs


def stream_b(w_in, w_proj_a, w_proj_b, w_out):
    start = {"v": 2048, "z": 3072, "V": 6144, "Z": 7168, "g": 8192, "G": 9216}
    slabs = np.zeros((LAYERS, len(UNITS_B), P, 2048), np.float32)
    for layer in range(LAYERS):
        for u, (kind, i) in enumerate(UNITS_B):
            two = [256 * i, 256 * i + P]
            if kind in start:
                s = tiles(w_in[layer], [start[kind] + c for c in two])
            elif kind == "qk":
                s = tiles(w_in[layer], [P * i, D + P * i])
            elif kind == "QK":
                s = tiles(w_in[layer], [4096 + P * i, 5120 + P * i])
            else:
                s = tiles({"pa": w_proj_a, "pb": w_proj_b, "out": w_out}[kind][layer], two)
            slabs[layer, u] = s
    return slabs


def columns(v, layers=LAYERS):
    return v.reshape(layers, -1, P).transpose(0, 2, 1)


def kernel(**inputs):
    import concourse.bacc as _bacc
    from concourse.bass_utils import run_bass_kernel_spmd as _run

    g = {k: np.asarray(v) for k, v in inputs.items()}
    common, const_a, const_b = constant_table()
    common[:, CC["final"]:][:, :KD] = g["norm_final"].reshape(KD, P).T
    common[:, CC["final"] + KD:][:, :KD] = g["final_norm_w_2"].reshape(KD, P).T
    vec_a = np.concatenate(
        [columns(g["norm_mix"]), columns(g["norm_ffn"]), columns(g["b_gate"]), columns(g["sc_conv"]),
         columns(g["rw_mu"]), columns(g["rw_w0"]), columns(g["rw_a0"]), columns(g["rw_k_k"]), columns(g["rw_k_a"]),
         columns(g["rw_r_k"]), columns(g["rw_ln_w"]), columns(g["rw_ln_b"]), columns(g["ffn_conv"])], 2)
    lora = np.concatenate([np.concatenate([g["rw_w_up"], g["rw_a_up"]], 1), g["rw_g_up"]], 2)
    lam = np.zeros((LAYERS, P, 4), np.float32)
    for c, name in enumerate(("lambda_q1_2", "lambda_k1_2", "lambda_q2_2", "lambda_k2_2")):
        lam[:, :HD, c] = g[name]
    lam_init = np.zeros((LAYERS, P, 2), np.float32)
    for layer in range(LAYERS):
        start = 0.8 - 0.6 * math.exp(-0.3 * layer)
        lam_init[layer] = (start, 1.0 - start)
    vec_b = np.concatenate([columns(g["norm_w_2"]), columns(g["subln_w_2"]), lam, lam_init], 2)
    arrays = {
        "x_t": g["x"][0].reshape(T, KD, P).transpose(2, 1, 0),
        "positions": g["positions"],
        "common": common, "const_a": const_a, "const_b": const_b,
        "vec_a": vec_a, "lora": lora, "vec_b": vec_b,
        "stream_a": stream_a(g["w_in"], g["w_branch"], g["w_out"], g["ffn_up"], g["ffn_down"]),
        "stream_b": stream_b(g["w_in_2"], g["w_proj_a_2"], g["w_proj_b_2"], g["w_out_2"]),
    }
    arrays = {k: np.ascontiguousarray(v) for k, v in arrays.items()}
    nc = _bacc.Bacc("TRN2", target_bir_lowering=False, num_devices=1)
    dram = {k: nc.dram_tensor(k, v.shape, mybir.dt.from_np(v.dtype), kind="ExternalInput").ap()
            for k, v in arrays.items()}
    out = nc.dram_tensor("out_t", (P, KD, T), F32, kind="ExternalOutput").ap()
    build(nc, dram, out)
    r = _run(nc, [arrays], core_ids=[0])
    got = r.results[0]["out_t"]
    return np.ascontiguousarray(got.transpose(2, 1, 0).reshape(1, T, D))
```
